# Optimizing a Trainium2 kernel written in Bass

```python
import math
import jax, jax.numpy as jnp
from jax import lax
import numpy as np

D_MODEL = 1024
BATCH = 1
SEQ = 512
DEPTH = 2
DEC_BATCH = 8
DEC_SEQ = 8
PAST_LEN = 2048
PAGE_SIZE = 128

N_MIXERS = 2
N_CONV = (DEPTH + 1) // 2
N_ATTN = DEPTH // 2
E_CONV = D_MODEL
CONV_WIDTH = 31
HEAD_DIM = 64
N_HEADS = D_MODEL // HEAD_DIM
E_ATTN = N_HEADS * HEAD_DIM
GROUPS = ((128, 1), (512, 4), (2048, 16))
N_GROUPS = len(GROUPS)
MAX_DIL = 16
Q_BLOCK = 128
ALPHA = (2.0 * DEPTH) ** 0.25
BETA = (8.0 * DEPTH) ** -0.25
LN_EPS = 1e-5
NEG_INF = -1e30

kernel_name = "gated_conformer_conv_dilated_swa_deepnorm_step"

def layer_norm(x, g, b):
    xf = x.astype(jnp.float32)
    mu = jnp.mean(xf, axis=-1, keepdims=True)
    var = jnp.mean(jnp.square(xf - mu), axis=-1, keepdims=True)
    y = (xf - mu) * lax.rsqrt(var + LN_EPS) * g.astype(jnp.float32) + b.astype(jnp.float32)
    return y.astype(x.dtype)

def conv_mixer(x, buf, w_in, dw_w, dw_b, ln_g, ln_b, w_out):
    h = jnp.einsum('btd,de->bte', x, w_in)
    a, gl, z = jnp.split(h, 3, axis=-1)
    u = a * jax.nn.sigmoid(gl)
    u_all = jnp.concatenate([buf.astype(u.dtype), u], axis=1)
    c = lax.conv_general_dilated(u_all, dw_w[:, None, :].astype(u.dtype), window_strides=(1,), padding='VALID',
                                 dimension_numbers=('NWC', 'WIO', 'NWC'), feature_group_count=E_CONV)
    c = layer_norm(c + dw_b, ln_g, ln_b)
    y = jax.nn.silu(c) * jax.nn.silu(z)
    out = jnp.einsum('bte,ed->btd', y, w_out)
    return out, u_all[:, -(CONV_WIDTH - 1):]

def dilated_group_attn(q, k_all, v_all, p0, window, dil, qb):
    B, t_pad, H, hd = q.shape
    nb = t_pad // qb
    n_k = (window + qb) // dil
    n_a = qb // dil
    jj = jnp.arange(n_k)[None, :]
    aa = jnp.arange(n_a)[:, None]
    band = (jj >= aa) & (jj <= aa + window // dil)
    slot = jnp.arange(n_k)[:, None] * dil + jnp.arange(dil)[None, :]
    scale = HEAD_DIM ** -0.5

    def block(b):
        start = b * qb
        qs = lax.dynamic_slice_in_dim(q, start, qb, axis=1).reshape(B, n_a, dil, H, hd)
        ks = lax.dynamic_slice_in_dim(k_all, start, window + qb, axis=1).reshape(B, n_k, dil, H, hd)
        vs = lax.dynamic_slice_in_dim(v_all, start, window + qb, axis=1).reshape(B, n_k, dil, H, hd)
        valid = (p0 - window + start + slot) >= 0
        mask = band[None, :, :] & valid.T[:, None, :]
        s = jnp.einsum('barhe,bjrhe->bhraj', qs, ks).astype(jnp.float32) * scale
        s = jnp.where(mask, s, NEG_INF)
        m = jnp.max(s, axis=-1, keepdims=True)
        p = jnp.exp(s - m)
        l = jnp.sum(p, axis=-1, keepdims=True)
        o = jnp.einsum('bhraj,bjrhe->barhe', (p / l).astype(vs.dtype), vs)
        lse = jnp.transpose((m + jnp.log(l))[..., 0], (0, 3, 2, 1))
        return o.reshape(B, qb, H, hd), lse.reshape(B, qb, H)

    o, lse = lax.map(block, jnp.arange(nb))
    o = jnp.moveaxis(o, 0, 1).reshape(B, t_pad, H, hd)
    lse = jnp.moveaxis(lse, 0, 1).reshape(B, t_pad, H)
    return o, lse

def dilated_attn_mixer(x, kv_bufs, p0, w_in, w_out):
    B, T, _ = x.shape
    h = jnp.einsum('btd,de->bte', x, w_in)
    n_qkv = 3 * N_GROUPS * E_ATTN
    qkv = h[..., :n_qkv].reshape(B, T, N_GROUPS, 3, N_HEADS, HEAD_DIM)
    z = h[..., n_qkv:]
    qb = Q_BLOCK if T >= Q_BLOCK else -(-T // MAX_DIL) * MAX_DIL
    t_pad = -(-T // qb) * qb
    q_pad = ((0, 0), (0, t_pad - T), (0, 0), (0, 0))
    outs, lses, new_kv = [], [], []
    for g, (window, dil) in enumerate(GROUPS):
        q, k, v = qkv[:, :, g, 0], qkv[:, :, g, 1], qkv[:, :, g, 2]
        if kv_bufs is None:
            k_ctx, v_ctx = k, v
        else:
            buf = kv_bufs[g].astype(k.dtype)
            k_ctx = jnp.concatenate([buf[:, :, 0], k], axis=1)
            v_ctx = jnp.concatenate([buf[:, :, 1], v], axis=1)
        keep = min(window, p0 + T)
        new_kv.append(jnp.stack([k_ctx[:, -keep:], v_ctx[:, -keep:]], axis=2))
        n_ctx = k_ctx.shape[1]
        kv_pad = ((0, 0), (window + T - n_ctx, t_pad - T), (0, 0), (0, 0))
        o, lse = dilated_group_attn(jnp.pad(q, q_pad), jnp.pad(k_ctx, kv_pad), jnp.pad(v_ctx, kv_pad),
                                    p0, window, dil, qb)
        outs.append(o[:, :T])
        lses.append(lse[:, :T])
    o = jnp.stack(outs, axis=2)
    wgt = jax.nn.softmax(jnp.stack(lses, axis=2), axis=2)
    o = jnp.einsum('btgh,btghe->bthe', wgt.astype(o.dtype), o).reshape(B, T, E_ATTN)
    y = jnp.einsum('bte,ed->btd', o * jax.nn.silu(z), w_out)
    return y, new_kv

def setup_inputs(seed: int = 0) -> dict:
    key = jax.random.key(seed)
    ks = jax.random.split(key, 20)
    f32 = jnp.float32
    nrm = lambda k, s: jax.random.normal(k, s, f32)
    kv_shape = lambda w: (N_ATTN, DEC_BATCH, min(w, PAST_LEN), 2, N_HEADS, HEAD_DIM)
    return {
        "x_prompt": nrm(ks[0], (BATCH, SEQ, D_MODEL)),
        "x_sample": nrm(ks[1], (DEC_BATCH, DEC_SEQ, D_MODEL)),
        "cache_kv_w128_d1": nrm(ks[2], kv_shape(GROUPS[0][0])),
        "cache_kv_w512_d4": nrm(ks[3], kv_shape(GROUPS[1][0])),
        "cache_kv_w2048_d16": nrm(ks[4], kv_shape(GROUPS[2][0])),
        "state_conv": 0.5 * nrm(ks[5], (N_CONV, DEC_BATCH, CONV_WIDTH - 1, E_CONV)),
        "conv_w_in": nrm(ks[6], (N_CONV, D_MODEL, 3 * E_CONV)) * D_MODEL ** -0.5,
        "conv_dw_w": nrm(ks[7], (N_CONV, CONV_WIDTH, E_CONV)) * CONV_WIDTH ** -0.5,
        "conv_dw_b": 0.02 * nrm(ks[8], (N_CONV, E_CONV)),
        "conv_ln_g": 1.0 + 0.02 * nrm(ks[9], (N_CONV, E_CONV)),
        "conv_ln_b": 0.02 * nrm(ks[10], (N_CONV, E_CONV)),
        "conv_w_out": nrm(ks[11], (N_CONV, E_CONV, D_MODEL)) * (E_CONV ** -0.5 * BETA),
        "attn_w_in": nrm(ks[12], (N_ATTN, D_MODEL, (3 * N_GROUPS + 1) * E_ATTN)) * D_MODEL ** -0.5,
        "attn_w_out": nrm(ks[13], (N_ATTN, E_ATTN, D_MODEL)) * (E_ATTN ** -0.5 * BETA),
        "norm_g": 1.0 + 0.02 * nrm(ks[14], (DEPTH, D_MODEL)),
        "norm_b": 0.02 * nrm(ks[15], (DEPTH, D_MODEL)),
    }

def reference(x_prompt, x_sample, cache_kv_w128_d1, cache_kv_w512_d4, cache_kv_w2048_d16, state_conv,
              conv_w_in, conv_dw_w, conv_dw_b, conv_ln_g, conv_ln_b, conv_w_out,
              attn_w_in, attn_w_out, norm_g, norm_b):
    caches = (cache_kv_w128_d1, cache_kv_w512_d4, cache_kv_w2048_d16)
    yp, ys = x_prompt, x_sample
    kv_p = [[] for _ in GROUPS]
    kv_s = [[] for _ in GROUPS]
    conv_p, conv_s = [], []
    for i in range(DEPTH):
        li = i // N_MIXERS
        if i % N_MIXERS == 0:
            prm = (conv_w_in[li], conv_dw_w[li], conv_dw_b[li], conv_ln_g[li], conv_ln_b[li], conv_w_out[li])
            zero_buf = jnp.zeros((yp.shape[0], CONV_WIDTH - 1, E_CONV), yp.dtype)
            fp, bp = conv_mixer(yp, zero_buf, *prm)
            fs, bs = conv_mixer(ys, state_conv[li], *prm)
            conv_p.append(bp)
            conv_s.append(bs)
        else:
            fp, nkp = dilated_attn_mixer(yp, None, 0, attn_w_in[li], attn_w_out[li])
            fs, nks = dilated_attn_mixer(ys, [c[li] for c in caches], PAST_LEN, attn_w_in[li], attn_w_out[li])
            for g in range(N_GROUPS):
                kv_p[g].append(nkp[g])
                kv_s[g].append(nks[g])
        yp = layer_norm(ALPHA * yp + fp, norm_g[i], norm_b[i])
        ys = layer_norm(ALPHA * ys + fs, norm_g[i], norm_b[i])
    return (yp, ys,
            jnp.stack(kv_p[0]), jnp.stack(kv_p[1]), jnp.stack(kv_p[2]), jnp.stack(conv_p),
            jnp.stack(kv_s[0]), jnp.stack(kv_s[1]), jnp.stack(kv_s[2]), jnp.stack(conv_s))


_drawn_inputs = setup_inputs


def setup_inputs(seed=0):
    import zlib

    import numpy as np

    out = dict(_drawn_inputs(seed))
    spreads = {}
    factors = {'conv_dw_b': 8.0, 'conv_ln_g': 8.0, 'conv_ln_b': 8.0}
    for name, (base, spread) in spreads.items():
        noise = np.random.default_rng([zlib.crc32(name.encode()), seed]).standard_normal(out[name].shape)
        drawn = base * np.exp(spread * noise) if base else spread * noise
        out[name] = __import__('jax').numpy.asarray(drawn.astype(out[name].dtype))
    for name, factor in factors.items():
        out[name] = (out[name] * factor).astype(out[name].dtype)
    return out
```

```python
from contextlib import ExitStack

import concourse.bass as bass
from concourse import mybir
import numpy as np

F32 = mybir.dt.float32
F32R = mybir.dt.float32r
ALU = mybir.AluOpType
ACT = mybir.ActivationFunctionType

P = 128
D = 1024
KC = D // P
SEQ = 512
NB = 8
NQ = 8
NS = NB * NQ
NT = NS + SEQ
NCL = 4
W = 31
HALO = W - 1
HD = 64
NG = 3
WIN = (128, 512, 2048)
DIL = (1, 4, 16)
HG = 4
TILES = 1 + 4 + 8
GROUP_OF = [0] + [1] * 4 + [2] * 8
SCALE = HD ** -0.5
ALPHA = 4.0 ** 0.25
EPS = 1e-5
NEG = -1e30

U_IN0 = 3 * KC
U_OUT0 = KC
U_CH = 10
U_HG = 2 * U_CH
N_OUT0 = U_IN0
N_IN1 = U_IN0 + U_OUT0
N_OUT1 = N_IN1 + HG * U_HG
UNITS = N_OUT1 + KC
LAND = 4
RING = 4
TILES_HG = 4 * TILES

T0 = 512 - NS - 2 * P
SPLIT = NS + 2 * P
V_DWB, V_LNG, V_LNB, V_G0, V_B0, V_G1, V_B1, V_EPS = range(W, W + 8)
NV = W + 8

SW = NG * P + NG * NS
PW = NCL * P + 2 * P
COPY_ROWS = (120, 252, 255)
COPY_RUNS = (16, 32, 32)
UW = HALO + SEQ + (HALO + NQ) * NB
US = HALO + SEQ

TAPS_EARLY = 16
CONV_OPS = 2 * W


def build(nc, d, o):
    with ExitStack() as ctx:
        def sb(name, shape, dt=F32, where=ctx):
            return where.enter_context(nc.sbuf_tensor(name, shape, dt))

        def sem(name):
            return ctx.enter_context(nc.semaphore(name))

        act_hi = sb("act_hi", [P, KC, NT], F32R)
        act_lo = sb("act_lo", [P, KC, NT], F32R)
        res = sb("res", [P, KC, NT])
        landing = sb("landing", [P, LAND, KC * P])
        w_hi = sb("w_hi", [P, 2, KC * P], F32R)
        w_lo = sb("w_lo", [P, 2, KC * P], F32R)
        ident = sb("ident_sb", [P, P])
        ones = sb("ones", [P, P])
        vec = sb("vec_sb", [P, KC, NV])
        mask_p = sb("mask_p_sb", [P, NCL, PW])
        mask_s = sb("mask_s_sb", [P, 2, SW])
        head_mask = sb("head_mask_sb", [P, 2 * P])
        pick = sb("pick_sb", [P, 4 * NQ])

        with ExitStack() as lay0:
            zs = sb("zs", [P, KC, NT], where=lay0)
            sg = sb("sg", [P, 2, NT], where=lay0)
            neg_mean = sb("neg_mean", [P, NT], where=lay0)
            std = sb("std", [P, NT], where=lay0)
            rstd = sb("rstd", [P, NT], where=lay0)
            sq = sb("sq", [P, 2, NT], where=lay0)
            with ExitStack() as early:
                u_in = sb("u_in", [P, KC, UW], where=early)
                prod = sb("prod", [P, W, NS], where=early)
            with ExitStack() as late:
                mid_hi = sb("mid_hi", [P, KC, NT], F32R, where=late)
                mid_lo = sb("mid_lo", [P, KC, NT], F32R, where=late)
        with ExitStack() as lay1:
            qT = sb("qT", [P, NG, NT], where=lay1)
            kT = sb("kT", [P, NG, NT], where=lay1)
            vT = sb("vT", [P, 2, NT], where=lay1)
            v_nat = sb("v_nat", [P, NG, NCL, P], where=lay1)
            zT = sb("zT", [P, NT], where=lay1)
            z_new = sb("z_new", [P, 2, NS], where=lay1)
            q_new = sb("q_new", [P, NG, 2, NS], where=lay1)
            k_new = sb("k_new", [P, NG, 2, NS], where=lay1)
            v_new = sb("v_new", [NS, NG, 2 * P], where=lay1)
            ring = sb("ring", [P, RING, 2 * 4 * P], where=lay1)
            probs = sb("probs", [P, 2, PW], where=lay1)
            probsT = sb("probsT", [P, 2, PW], where=lay1)
            q_row = sb("q_row", [P, 2, TILES + 2, 2, 4, 4, NQ], where=lay1)
            p_col = sb("p_col", [P, TILES, P], where=lay1)
            p_new = sb("p_new", [NS, NG, P], where=lay1)
            o_own = sb("o_own", [P, 2 * P], where=lay1)
            top = sb("top", [P, 2], where=lay1)
            neg_top = sb("neg_top", [P, 2], where=lay1)
            total = sb("total", [P, 2], where=lay1)
            share = sb("share", [P, 2], where=lay1)

        pair = [ctx.enter_context(nc.psum_tensor(f"pair{x}", [P, 1024], F32)) for x in "ABCD"]
        A, B, C, DD = pair

        consts_in = [sem(f"consts_in{i}") for i in range(6)]
        x_in = sem("x_in")
        state_in = sem("state_in")
        w_landed = [sem(f"w_landed{s}") for s in range(LAND)]
        w_split = sem("w_split")
        hi_done = sem("hi_done")
        proj_done = sem("proj_done")
        x_hi = sem("x_hi")
        x_split = sem("x_split")
        made = sem("made")
        gate_done = sem("gate_done")
        z_done = sem("z_done")
        u_done = sem("u_done")
        prod_done = sem("prod_done")
        conv = sem("conv")
        sconv = sem("sconv")
        ln_sum = sem("ln_sum")
        ln_mean = sem("ln_mean")
        ln_cent = sem("ln_cent")
        ln_sq = sem("ln_sq")
        ln_sqsum = sem("ln_sqsum")
        ln_std = sem("ln_std")
        ln_rstd = sem("ln_rstd")
        ln_scaled = sem("ln_scaled")
        ln_act = sem("ln_act")
        gated = sem("gated")
        mid_hi_done = sem("mid_hi_done")
        mid_split = sem("mid_split")
        res_part = sem("res_part")
        res_done = sem("res_done")
        qkv_out = sem("qkv_out")
        vt_done = sem("vt_done")
        v_ready = sem("v_ready")
        s_done = sem("s_done")
        s_max = sem("s_max")
        s_neg = sem("s_neg")
        s_exp = sem("s_exp")
        s_share = sem("s_share")
        s_norm = sem("s_norm")
        pt_done = sem("pt_done")
        pt_out = sem("pt_out")
        o_done = sem("o_done")
        o_out = sem("o_out")
        rows_cleared = sem("rows_cleared")
        q_rows = sem("q_rows")
        tile_in = [sem(f"tile_in{s}") for s in range(RING)]
        tile_used = sem("tile_used")
        ss_max = sem("ss_max")
        ss_neg = sem("ss_neg")
        ss_exp = sem("ss_exp")
        ss_share = sem("ss_share")
        ss_norm = sem("ss_norm")
        spt_done = sem("spt_done")
        p_cols = sem("p_cols")
        so_own = sem("so_own")
        sot_done = sem("sot_done")
        sot_out = sem("sot_out")
        k_stored = [sem(f"k_stored{g}") for g in range(NG)]
        v_stored = [sem(f"v_stored{s}") for s in range(2)]
        u_stored = sem("u_stored")
        y_stored = sem("y_stored")
        copied = sem("copied")

        block = ctx.enter_context(nc.Block())

        def tok(x, lo=0, hi=NT):
            return pair[x][:, T0 + lo:T0 + hi]

        @block.sync
        def _(sp):
            def load_unit(n, slot):
                sp.wait_ge(w_split, n + 1)
                sp.dma_start(landing[:, slot, :], d["w_units"][bass.ds(n, 1)].rearrange("a p m -> (a p) m"))\
                    .then_inc(w_landed[slot], 16)

            def copy_rows(g, b, piece):
                n = COPY_ROWS[g] * 2 * D
                src = d[f"cache{g}"][bass.ds(b, 1), (piece * n + NQ * 2 * D):(piece * n + NQ * 2 * D + n)]
                dst = o[f"kept{g}"][bass.ds(b, 1), piece * n:piece * n + n]
                sp.dma_start(dst.rearrange("a (r m) -> (a r) m", r=COPY_RUNS[g]),
                             src.rearrange("a (r m) -> (a r) m", r=COPY_RUNS[g])).then_inc(copied, 16)

            def store_u(j):
                sp.wait_ge(u_done, 2 * j + 4)
                sp.wait_ge(state_in, 16)
                sp.dma_start(o["conv_p"][:, j, :], u_in[:, j, SEQ:SEQ + HALO]).then_inc(u_stored, 16)
                sp.dma_start(o["conv_s"][:, j, :], u_in[:, j, US + NQ * NB:UW]).then_inc(u_stored, 16)

            for h in range(2):
                sp.dma_start(res[:, 4 * h:4 * h + 4, :], d["xT"][:, 4 * h:4 * h + 4, :]).then_inc(x_in, 16)
                if h == 0:
                    sp.wait_ge(x_in, 16)
            sp.wait_ge(made, 6)
            for n in range(LAND):
                load_unit(n, n)
            for i, (dst, name) in enumerate(((vec[:, :, :], "vec"), (ident[:, :], "ident"), (mask_p[:, :, :], "mask_p"),
                                             (mask_s[:, :, :], "mask_s"), (head_mask[:, :], "head_mask"),
                                             (pick[:, :], "pick"))):
                sp.dma_start(dst, d[name]).then_inc(consts_in[i], 16)
            sp.dma_start(u_in[:, :, US:US + HALO * NB], d["state"]).then_inc(state_in, 16)

            for j in range(KC):
                for i in range(3):
                    load_unit(3 * j + i + LAND, (3 * j + i) % LAND)
                    copy_rows(2, j, i)
                if j:
                    store_u(j - 1)
            store_u(KC - 1)
            with sp.Fori(0, 2) as it:
                for m in range(4):
                    load_unit(N_OUT0 + it * 4 + m + LAND, m)
                    copy_rows(2, it * 4 + m, 3)
                    copy_rows(1, it * 4 + m, 0)
                    copy_rows(1, it * 4 + m, 1)
            with sp.Fori(0, HG) as hg:
                for m in range(U_HG):
                    ch, i = divmod(m, U_CH)
                    load_unit(N_IN1 + hg * U_HG + m + LAND, m % LAND)
                    if i == 4:
                        copy_rows(0, hg * 2 + ch, 0)
                    if i in (1, 3, 5, 7):
                        copy_rows(2, hg * 2 + ch, 4 + i // 2)
                    if i and i % 3 != 1:
                        g, kv = (i - 1) // 3, (i - 1) % 3 - 1
                        sp.wait_ge(qkv_out, hg * U_HG + m)
                        sp.dma_start(o["kv_new"][bass.ds((hg * 2 + ch) * 6 + g * 2 + kv, 1)]
                                     .rearrange("a p n -> (a p) n"), kT[:, g, :] if kv == 0 else vT[:, g % 2, :])\
                            .then_inc(k_stored[g] if kv == 0 else v_stored[g % 2], 16)
                for t in range(TILES_HG):
                    sp.wait_ge(tile_used, hg * TILES_HG + t + 1)
                    if t == 0:
                        sp.wait_ge(qkv_out, U_HG)
                    which, tt = divmod(t, TILES)
                    src = d["k_tiles" if which < 2 else "v_tiles"]
                    sp.dma_start(ring[:, t % RING, :],
                                 src[bass.ds((hg * 2 + which % 2) * TILES + tt, 1)].rearrange("a p m -> (a p) m"))\
                        .then_inc(tile_in[t % RING], 16)
            for n in range(N_OUT1 + LAND, UNITS):
                load_unit(n, n % LAND)
            for k in range(KC):
                sp.wait_ge(ln_act, 2 * KC + k + 1)
                sp.dma_start(o["yT"][:, k, :], res[:, k, :]).then_inc(y_stored, 16)
            sp.wait_ge(copied, 16 * NB * (1 + 2 + 8))
            for g in range(NG):
                sp.wait_ge(k_stored[g], 16 + 16 * KC)
            sp.wait_ge(v_stored[0], 16 + 16 * 2 * KC)
            sp.wait_ge(v_stored[1], 16 + 16 * KC)
            sp.wait_ge(u_stored, 16 * 2 * KC)
            sp.wait_ge(y_stored, 16 * KC)

        @block.tensor
        def _(pe):
            def unit(n, s, src_hi, src_lo):
                pe.wait_ge(w_split, LAND + n + 1)
                for k in range(KC):
                    for q, (w, x) in enumerate(((w_hi, src_hi), (w_hi, src_lo), (w_lo, src_hi))):
                        first, last = k == 0 and q == 0, k == KC - 1 and q == 2
                        lhs = w[:, s, k * P:(k + 1) * P]
                        pe.matmul(tok(s, 0, SPLIT), lhs, x[:, k, 0:SPLIT], start=first, stop=last)
                        mm = pe.matmul(tok(s, SPLIT, NT), lhs, x[:, k, SPLIT:NT], start=first, stop=last)
                mm.then_inc(proj_done, 1)

            def norm_sums(round_):
                if round_ == 0:
                    pe.wait_ge(conv, CONV_OPS * KC // 2)
                    pe.wait_ge(sconv, 2 * KC)
                for k in range(KC):
                    if round_:
                        pe.wait_ge(res_done, KC * (round_ - 1) + k + 1)
                    pe.matmul(tok(2, 0, SPLIT), ones[:, :], res[:, k, 0:SPLIT], start=k == 0, stop=k == KC - 1)
                    mm = pe.matmul(tok(2, SPLIT, NT), ones[:, :], res[:, k, SPLIT:NT], start=k == 0, stop=k == KC - 1)
                mm.then_inc(ln_sum, 1)
                for k in range(KC):
                    pe.wait_ge(ln_sq, KC * round_ + k + 1)
                    pe.matmul(tok(3, 0, SPLIT), ones[:, :], sq[:, k % 2, 0:SPLIT], start=k == 0, stop=k == KC - 1)
                    pe.matmul(tok(3, SPLIT, NT), ones[:, :], sq[:, k % 2, SPLIT:NT], start=k == 0,
                              stop=k == KC - 1).then_inc(ln_sqsum, 1)

            pe.wait_ge(made, 6)
            pe.wait_ge(x_split, KC)
            with pe.Fori(0, 2) as it:
                for jj in range(4):
                    for i in range(3):
                        if i == 0:
                            pe.wait_ge(u_done, (it * 4 + jj) * 2 + 2)
                        elif i == 1:
                            pe.wait_ge(z_done, it * 4 + jj + 1)
                        else:
                            pe.wait_ge(gate_done, it * 4 + jj + 1)
                        unit(it * 12 + 3 * jj + i, (3 * jj + i) % 2, act_hi, act_lo)
            norm_sums(0)
            pe.wait_ge(z_done, 1 + KC)
            pe.wait_ge(mid_split, KC)
            with pe.Fori(0, 2) as it:
                for m in range(4):
                    pe.wait_ge(res_part, it * 4 + m + 1)
                    unit(N_OUT0 + it * 4 + m, m % 2, mid_hi, mid_lo)
            norm_sums(1)
            pe.wait_ge(x_split, 2 * KC)
            for i in range(1, 6):
                pe.wait_ge(consts_in[i], 16)

            with pe.Fori(0, HG) as hg:
                def v_turn(ch, g):
                    pe.wait_ge(qkv_out, hg * U_HG + ch * U_CH + 3 * g + 3)
                    if ch or g:
                        pe.wait_ge(v_ready, (hg * 2 + ch) * 6 + 2 * g)
                    if ch and g == 0:
                        pe.wait_ge(o_out, (hg * 2 + ch) * 4)
                    for c in range(NCL):
                        pe.transpose(DD[:, c * P:(c + 1) * P], vT[:, g % 2, NS + c * P:NS + (c + 1) * P], ident[:, :])
                    pe.transpose(DD[0:NS, 512:512 + P], vT[:, g % 2, 0:NS], ident[:, :]).then_inc(vt_done, 1)

                def scores(ch, u):
                    r, h = divmod(u, 2)
                    rows = slice(HD * h, HD * h + HD)
                    own = slice(NS + r * P, NS + (r + 1) * P)
                    S = pair[u % 2]
                    if u < 2:
                        pe.wait_ge(qkv_out, hg * U_HG + ch * U_CH + 9 + u)
                    else:
                        pe.wait_ge(s_max, (hg * 2 + ch) * 8 + u - 1)
                    pe.matmul(S[:, 0:512], qT[rows, 0, own], kT[rows, 0, NS:NT], start=True, stop=True)
                    pe.matmul(S[:, 512:640], qT[rows, 1, own], kT[rows, 1, own], start=True, stop=True)
                    pe.matmul(S[:, 640:768], qT[rows, 2, own], kT[rows, 2, own], start=True, stop=True)\
                        .then_inc(s_done, 1)

                def turn_probs(ch, u):
                    su = (hg * 2 + ch) * 8 + u
                    pe.wait_ge(s_norm, su + 1)
                    if ch or u:
                        pe.wait_ge(pt_out, su)
                    for c in range(6):
                        mm = pe.transpose(C[:, c * P:(c + 1) * P], probs[:, u % 2, c * P:(c + 1) * P], ident[:, :])
                    mm.then_inc(pt_done, 1)

                def mix(ch, r):
                    pe.wait_ge(pt_out, (hg * 2 + ch) * 8 + 2 * r + 2)
                    if r == 0:
                        pe.wait_ge(v_ready, (hg * 2 + ch) * 6 + 6)
                    else:
                        pe.wait_ge(o_out, (hg * 2 + ch) * 4 + r)
                    for c in range(6):
                        v = v_nat[:, 0, c, :] if c < 4 else v_nat[:, c - 3, r, :]
                        for h in range(2):
                            mm = pe.matmul(DD[HD * h:HD * h + HD, 0:P], v[:, HD * h:HD * h + HD],
                                           probsT[:, h, c * P:(c + 1) * P], start=c == 0, stop=c == 5)
                    mm.then_inc(o_done, 1)

                for ch in range(2):
                    for i in range(U_CH):
                        m = ch * U_CH + i
                        if i >= 2:
                            pe.wait_ge(qkv_out, hg * U_HG + m - 1)
                        unit(N_IN1 + hg * U_HG + m, m % 2, act_hi, act_lo)
                        if i in (3, 6, 9):
                            v_turn(ch, i // 3 - 1)
                    scores(ch, 0)
                    scores(ch, 1)
                    for r in range(NCL):
                        turn_probs(ch, 2 * r)
                        if r < NCL - 1:
                            scores(ch, 2 * r + 2)
                        turn_probs(ch, 2 * r + 1)
                        if r < NCL - 1:
                            scores(ch, 2 * r + 3)
                        mix(ch, r)

                def tile_ready(t):
                    pe.wait_ge(tile_in[t % RING], (hg * (TILES_HG // RING) + t // RING + 1) * 16)

                def score_rows(bh, t, S, cols, first, last, keys):
                    for ch in range(2):
                        for b in range(4):
                            mm = pe.matmul(S[32 * b:32 * b + 32, cols],
                                           q_row[:, bh, t, ch, b, :, :].rearrange("p h q -> p (h q)"),
                                           keys(ch, b), start=first and ch == 0, stop=last and ch == 1)
                    return mm

                for bh in range(2):
                    S = pair[2 + bh]
                    pe.wait_ge(q_rows, hg * 2 + bh + 1)
                    pe.wait_ge(o_out, (hg + 1) * 8)
                    for g in range(NG):
                        score_rows(bh, (0, TILES, TILES + 1)[g], S, slice(512 + g * NS, 512 + (g + 1) * NS), True, True,
                                   lambda ch, b: k_new[:, g, ch, :])
                    for t in range(TILES):
                        tt = bh * TILES + t
                        tile_ready(tt)
                        g = GROUP_OF[t]
                        kt = ring[:, tt % RING, :].rearrange("p (c b n) -> p c b n", c=2, b=4)
                        mm = score_rows(bh, t, S, slice(P + g * P, P + (g + 1) * P), t in (0, 1, 5),
                                        t in (0, 4, 12), lambda ch, b: kt[:, ch, b, :])
                        mm.then_inc(tile_used, 1)

                for bh in range(2):
                    T, O = pair[bh], pair[2 + bh]
                    pe.wait_ge(ss_norm, hg * 2 + bh + 1)
                    for g in range(NG):
                        pe.transpose(T[:, g * P:(g + 1) * P], probs[:, bh, g * P:(g + 1) * P], ident[:, :])
                    for g in range(NG):
                        mm = pe.transpose(T[0:NS, 512 + g * P:512 + (g + 1) * P],
                                          probs[:, bh, NG * P + g * NS:NG * P + (g + 1) * NS], ident[:, :])
                    mm.then_inc(spt_done, 1)
                    pe.wait_ge(p_cols, (hg * 2 + bh + 1) * (2 + NG))
                    for t in range(TILES):
                        tt = (2 + bh) * TILES + t
                        tile_ready(tt)
                        for b in range(4):
                            mm = pe.matmul(O[32 * b:32 * b + 32, 0:2 * P], p_col[:, t, 32 * b:32 * b + 32],
                                           ring[:, tt % RING, b * 2 * P:(b + 1) * 2 * P],
                                           start=t == 0, stop=t == TILES - 1)
                        mm.then_inc(tile_used, 1)
                        for g in range(NG if t == 0 else 0):
                            for b in range(4):
                                pe.matmul(O[32 * b:32 * b + 32, 0:2 * P], p_new[:, g, 32 * b:32 * b + 32],
                                          v_new[:, g, :], start=False, stop=False)
                    pe.wait_ge(so_own, hg * 2 + bh + 1)
                    for ch in range(2):
                        mm = pe.matmul(T[:, ch * 4 * NQ:(ch + 1) * 4 * NQ], o_own[:, ch * P:(ch + 1) * P], pick[:, :],
                                       start=True, stop=True)
                    mm.then_inc(sot_done, 1)
                pe.wait_ge(sot_out, (hg + 1) * 4)

            pe.wait_ge(mid_split, 2 * KC)
            with pe.Fori(0, 2) as it:
                for m in range(4):
                    pe.wait_ge(res_part, KC + it * 4 + m + 1)
                    unit(N_OUT1 + it * 4 + m, m % 2, mid_hi, mid_lo)
            norm_sums(2)

        @block.scalar
        def _(act):
            def split_hi(base, it, per, m):
                n = base + it * per + m
                act.wait_ge(w_landed[m % LAND], (base // LAND + it * (per // LAND) + m // LAND + 1) * 16)
                if m >= 2:
                    act.wait_ge(proj_done, n - 1)
                act.activation(w_hi[:, m % 2, :], landing[:, m % LAND, :], ACT.Copy).then_inc(hi_done, 1)

            def norm(round_):
                act.wait_ge(ln_sum, round_ + 1)
                act.activation(neg_mean[:, :], tok(2), ACT.Copy, scale=-1.0 / D).then_inc(ln_mean, 1)
                for k in range(KC):
                    act.wait_ge(ln_cent, KC * round_ + k + 1)
                    if k >= 2:
                        act.wait_ge(ln_sqsum, KC * round_ + k - 1)
                    act.activation(sq[:, k % 2, :], res[:, k, :], ACT.Square).then_inc(ln_sq, 1)
                act.wait_ge(ln_sqsum, KC * (round_ + 1))
                act.activation(std[:, :], tok(3), ACT.Sqrt, scale=1.0 / D, bias=vec[:, 0, V_EPS:V_EPS + 1]).then_inc(ln_std, 1)

            for k in range(KC):
                if k % 4 == 0:
                    act.wait_ge(x_in, 16 * (k // 4 + 1))
                act.activation(act_hi[:, k, :], res[:, k, :], ACT.Copy).then_inc(x_hi, 1)
            split_hi(0, 0, 0, 0)
            split_hi(0, 0, 0, 1)
            with act.Fori(0, 2) as it:
                for jj in range(4):
                    for i in range(3):
                        m = 3 * jj + i
                        split_hi(0, it, 12, m + 2)
                        if i == 0:
                            act.wait_ge(proj_done, it * 12 + m + 1)
                            act.activation(sg[:, jj % 2, :], tok(m % 2), ACT.Sigmoid).then_inc(gate_done, 1)
                        if i == 2:
                            act.wait_ge(proj_done, it * 12 + m + 1)
                            act.activation(zs[:, bass.ds(it * 4 + jj, 1), :].rearrange("p a n -> p (a n)"),
                                           tok(m % 2), ACT.Silu).then_inc(z_done, 1)
            act.wait_ge(consts_in[0], 16)
            norm(0)
            act.wait_ge(u_stored, 16 * 2 * KC)
            for k in range(KC + 1):
                if k < KC:
                    act.wait_ge(ln_scaled, k + 1)
                    if k >= 2:
                        act.wait_ge(gated, 2 * (k - 1))
                    act.activation(sg[:, k % 2, :], res[:, k, :], ACT.Silu, bias=vec[:, k, V_LNB:V_LNB + 1],
                                   scale=vec[:, k, V_LNG:V_LNG + 1]).then_inc(ln_act, 1)
                if k:
                    act.wait_ge(gated, 2 * k)
                    act.activation(mid_hi[:, k - 1, :], res[:, k - 1, :], ACT.Copy).then_inc(mid_hi_done, 1)
            with act.Fori(0, 2) as it:
                for m in range(4):
                    split_hi(N_OUT0, it, 4, m + 2)
            norm(1)
            for k in range(KC):
                act.wait_ge(ln_scaled, KC + k + 1)
                act.activation(res[:, k, :], res[:, k, :], ACT.Identity, bias=vec[:, k, V_B0:V_B0 + 1],
                               scale=vec[:, k, V_G0:V_G0 + 1]).then_inc(ln_act, 1)
                act.wait_ge(ln_act, KC + k + 1)
                act.activation(act_hi[:, k, :], res[:, k, :], ACT.Copy).then_inc(x_hi, 1)

            with act.Fori(0, HG) as hg:
                for ch in range(2):
                    chunk = hg * 2 + ch
                    for i in range(U_CH):
                        m = ch * U_CH + i
                        g, kind = divmod(i, 3)
                        split_hi(N_IN1, hg, U_HG, m + 2)
                        act.wait_ge(proj_done, N_IN1 + hg * U_HG + m + 1)
                        kept = (z_new[:, ch, :] if i == U_CH - 1 else q_new[:, g, ch, :] if kind == 0 else
                                k_new[:, g, ch, :] if kind == 1 else None)
                        if kept is not None:
                            act.activation(kept, tok(m % 2, 0, NS), ACT.Silu if i == U_CH - 1 else ACT.Copy)
                        if i == U_CH - 1:
                            act.activation(zT[:, :], tok(m % 2), ACT.Silu).then_inc(qkv_out, 1)
                        elif kind == 0:
                            act.activation(qT[:, g, :], tok(m % 2), ACT.Copy).then_inc(qkv_out, 1)
                        elif kind == 1:
                            act.wait_ge(k_stored[g], 16 + 16 * chunk)
                            act.activation(kT[:, g, :], tok(m % 2), ACT.Copy).then_inc(qkv_out, 1)
                        else:
                            act.wait_ge(v_stored[g % 2], 16 + 16 * (chunk if g == 1 else chunk * 2 + g // 2))
                            act.activation(vT[:, g % 2, :], tok(m % 2), ACT.Copy).then_inc(qkv_out, 1)

                    def exp(u):
                        act.wait_ge(s_neg, chunk * 8 + u + 1)
                        act.activation(probs[:, u % 2, :], probs[:, u % 2, :], ACT.Exp, scale=SCALE,
                                       bias=neg_top[:, u % 2:u % 2 + 1],
                                       accum_out=total[:, u % 2:u % 2 + 1]).then_inc(s_exp, 1)

                    def probs_out(u):
                        act.wait_ge(pt_done, chunk * 8 + u + 1)
                        if u >= 2:
                            act.wait_ge(o_done, chunk * 4 + u // 2)
                        act.activation(probsT[:, u % 2, :], C[:, 0:PW], ACT.Copy).then_inc(pt_out, 1)

                    exp(0)
                    exp(1)
                    for r in range(NCL):
                        for h in range(2):
                            probs_out(2 * r + h)
                            if r < NCL - 1:
                                exp(2 * r + 2 + h)
                for bh in range(2):
                    act.wait_ge(ss_neg, hg * 2 + bh + 1)
                    act.activation(probs[:, bh, 0:SW], probs[:, bh, 0:SW], ACT.Exp, scale=SCALE,
                                   bias=neg_top[:, bh:bh + 1], accum_out=total[:, bh:bh + 1]).then_inc(ss_exp, 1)

            act.wait_ge(sot_out, HG * 4)
            for k in range(KC):
                act.activation(mid_hi[:, k, :], res[:, k, :], ACT.Copy).then_inc(mid_hi_done, 1)
            for m in range(2, KC):
                split_hi(N_OUT1, 0, 0, m)
            norm(2)
            for k in range(KC):
                act.wait_ge(ln_scaled, 2 * KC + k + 1)
                act.activation(res[:, k, :], res[:, k, :], ACT.Identity, bias=vec[:, k, V_B1:V_B1 + 1],
                               scale=vec[:, k, V_G1:V_G1 + 1]).then_inc(ln_act, 1)

        @block.gpsimd
        def _(pool):
            def lo(dst, src, hi):
                return pool.tensor_tensor(dst, src, hi.bitcast(F32), ALU.subtract)

            def split_lo(base, it, per, m):
                pool.wait_ge(hi_done, base + it * per + m + 1)
                lo(w_lo[:, m % 2, :], landing[:, m % LAND, :], w_hi[:, m % 2, :]).then_inc(w_split, 1)

            pool.memset(ones[:, :], 1.0).then_inc(made, 1)
            pool.sem_inc(w_split, LAND)
            pool.sem_inc(z_done, 1)
            pool.sem_inc(u_done, 2)
            pool.sem_inc(res_part, 2)
            pool.sem_inc(tile_used, RING)
            for s in (*k_stored, *v_stored):
                pool.sem_inc(s, 16)
            pool.memset(u_in[:, :, 0:HALO], 0.0).then_inc(made, 5)
            pool.wait_ge(made, 6)

            for k in range(KC):
                pool.wait_ge(x_hi, k + 1)
                lo(act_lo[:, k, :], res[:, k, :], act_hi[:, k, :]).then_inc(x_split, 1)
            split_lo(0, 0, 0, 0)
            split_lo(0, 0, 0, 1)
            for j in range(KC):
                for i in range(3):
                    split_lo(0, 0, 0, 3 * j + i + 2)
                if j == 0:
                    pool.wait_ge(state_in, 16)
                    pool.wait_ge(consts_in[0], 16)
                else:
                    pool.wait_ge(sconv, 2 * j - 1)
                pool.wait_ge(u_done, 2 * j + 4)
                first = u_in[:, j, US:US + NS]
                windows = bass.AP(tensor=first.tensor, offset=first.offset, ap=[first.ap[0], [NB, W], [1, NS]])
                taps = vec[:, j, 0:W].unsqueeze(2).to_broadcast([P, W, NS])
                pool.tensor_tensor(prod[:, :, :], windows, taps, ALU.mult).then_inc(prod_done, 1)
            for k in range(KC):
                pool.wait_ge(mid_hi_done, k + 1)
                lo(mid_lo[:, k, :], res[:, k, :], mid_hi[:, k, :]).then_inc(mid_split, 1)
            with pool.Fori(0, 2) as it:
                for m in range(4):
                    split_lo(N_OUT0, it, 4, m + 2)
            for k in range(KC):
                pool.wait_ge(x_hi, KC + k + 1)
                lo(act_lo[:, k, :], res[:, k, :], act_hi[:, k, :]).then_inc(x_split, 1)
            pool.wait_ge(x_split, 2 * KC)
            pool.memset(q_row[:, :, :, :, :, :, :], 0.0).then_inc(rows_cleared, 1)
            pool.memset(p_col[:, :, :], 0.0).then_inc(rows_cleared, 1)
            with pool.Fori(0, HG) as hg:
                for ch in range(2):
                    for i in range(U_CH):
                        split_lo(N_IN1, hg, U_HG, ch * U_CH + i + 2)
            for k in range(KC):
                pool.wait_ge(mid_hi_done, KC + k + 1)
                lo(mid_lo[:, k, :], res[:, k, :], mid_hi[:, k, :]).then_inc(mid_split, 1)
            for m in range(2, KC):
                split_lo(N_OUT1, 0, 0, m)

        @block.vector
        def _(dve):
            def by_class(x):
                return x.rearrange("p (i c) -> p c i", c=NCL)

            def of_class(x):
                return x.rearrange("p (c i) -> p c i", c=NCL)

            def value(j):
                s = (3 * j + 1) % 2
                dve.wait_ge(proj_done, 3 * j + 2)
                dve.wait_ge(gate_done, j + 1)
                dve.tensor_tensor(u_in[:, j, US + HALO * NB:UW], tok(s, 0, NS), sg[:, j % 2, 0:NS], ALU.mult)\
                    .then_inc(u_done, 1)
                dve.tensor_tensor(by_class(u_in[:, j, HALO:US]), of_class(tok(s, NS, NT)), of_class(sg[:, j % 2, NS:NT]),
                                  ALU.mult).then_inc(u_done, 1)

            def taps(pair_, lo_, hi_):
                for w in range(lo_, hi_):
                    for a in range(2):
                        j, q = 2 * pair_ + a, pair_ * CONV_OPS + 2 * w + a
                        x, acc = u_in[:, j, w:w + SEQ], res[:, j, NS:NT]
                        if w == 0:
                            dve.tensor_scalar(acc, x, vec[:, j, 0:1], vec[:, j, V_DWB:V_DWB + 1], ALU.mult, ALU.add)\
                                .then_inc(conv, 1)
                        else:
                            dve.wait_ge(conv, q - 1)
                            dve.scalar_tensor_tensor(out=acc, in0=x, scalar=vec[:, j, w:w + 1], in1=acc,
                                                     op0=ALU.mult, op1=ALU.add).then_inc(conv, 1)

            def sample_taps(j):
                dve.wait_ge(prod_done, j + 1)
                dve.tensor_reduce(res[:, j, 0:NS], prod[:, :, :].rearrange("p w n -> p n w"), mybir.AxisListType.X,
                                  ALU.add).then_inc(sconv, 1)
                dve.wait_ge(sconv, 2 * j + 1)
                dve.tensor_scalar(res[:, j, 0:NS], res[:, j, 0:NS], vec[:, j, V_DWB:V_DWB + 1], None, ALU.add)\
                    .then_inc(sconv, 1)

            def norm(round_):
                dve.wait_ge(ln_mean, round_ + 1)
                for k in range(KC):
                    dve.tensor_tensor(res[:, k, :], res[:, k, :], neg_mean[:, :], ALU.add).then_inc(ln_cent, 1)
                dve.wait_ge(ln_std, round_ + 1)
                dve.reciprocal(rstd[:, :], std[:, :]).then_inc(ln_rstd, 1)
                dve.wait_ge(ln_rstd, round_ + 1)
                for k in range(KC):
                    dve.tensor_tensor(res[:, k, :], res[:, k, :], rstd[:, :], ALU.mult).then_inc(ln_scaled, 1)

            def residual(it, m, base, round_):
                at = bass.ds(it * 4 + m, 1)
                flat = lambda x: x[:, at, :].rearrange("p a n -> p (a n)")
                n = KC * round_ + it * 4 + m
                dve.wait_ge(proj_done, base + it * 4 + m + 1)
                dve.scalar_tensor_tensor(out=flat(res), in0=flat(act_hi).bitcast(F32), scalar=ALPHA, in1=tok(m % 2),
                                         op0=ALU.mult, op1=ALU.add).then_inc(res_part, 1)
                dve.wait_ge(res_part, n + 3)
                dve.scalar_tensor_tensor(out=flat(res), in0=flat(act_lo).bitcast(F32), scalar=ALPHA, in1=flat(res),
                                         op0=ALU.mult, op1=ALU.add).then_inc(res_done, 1)

            dve.wait_ge(made, 6)
            dve.wait_ge(consts_in[0], 16)
            dve.wait_ge(x_split, KC)
            value(0)
            value(1)
            for p in range(KC // 2):
                dve.wait_ge(u_done, 2 + 4 * (p + 1))
                taps(p, 0, TAPS_EARLY)
                if p < KC // 2 - 1:
                    value(2 * p + 2)
                sample_taps(2 * p)
                taps(p, TAPS_EARLY, W)
                if p < KC // 2 - 1:
                    value(2 * p + 3)
                sample_taps(2 * p + 1)
            norm(0)
            for k in range(KC):
                dve.wait_ge(ln_act, k + 1)
                dve.tensor_tensor(res[:, k, 0:NS], sg[:, k % 2, 0:NS], zs[:, k, 0:NS], ALU.mult).then_inc(gated, 1)
                dve.tensor_tensor(of_class(res[:, k, NS:NT]), by_class(sg[:, k % 2, NS:NT]), of_class(zs[:, k, NS:NT]),
                                  ALU.mult).then_inc(gated, 1)
            with dve.Fori(0, 2) as it:
                for m in range(4):
                    residual(it, m, N_OUT0, 0)
            norm(1)

            for i in range(1, 6):
                dve.wait_ge(consts_in[i], 16)
            dve.wait_ge(rows_cleared, 2)
            with dve.Fori(0, HG) as hg:
                def v_out(ch, g):
                    dve.wait_ge(vt_done, (hg * 2 + ch) * NG + g + 1)
                    dve.tensor_copy(v_nat[:, g, :, :].rearrange("p c n -> p (c n)"), DD[:, 0:512]).then_inc(v_ready, 1)
                    dve.tensor_copy(v_new[:, g, ch * P:(ch + 1) * P], DD[0:NS, 512:512 + P]).then_inc(v_ready, 1)

                def largest(chunk, u):
                    su, s = chunk * 8 + u, u % 2
                    dve.wait_ge(s_done, su + 1)
                    if u >= 2:
                        dve.wait_ge(pt_done, su - 1)
                    dve.memset(neg_top[:, s:s + 1], 0.0)
                    dve.tensor_tensor_reduce(probs[:, s, :], pair[s][:, 0:PW], mask_p[:, u // 2, :], 1.0, NEG, ALU.add,
                                             ALU.max, top[:, s:s + 1]).then_inc(s_max, 1)
                    dve.wait_ge(s_max, su + 1)
                    dve.tensor_scalar(neg_top[:, s:s + 1], top[:, s:s + 1], -SCALE, None, ALU.mult).then_inc(s_neg, 1)

                def normalise(chunk, u):
                    su, s = chunk * 8 + u, u % 2
                    dve.wait_ge(s_exp, su + 1)
                    dve.reciprocal(share[:, s:s + 1], total[:, s:s + 1]).then_inc(s_share, 1)
                    dve.wait_ge(s_share, su + 1)
                    dve.tensor_scalar(probs[:, s, :], probs[:, s, :], share[:, s:s + 1], None, ALU.mult)\
                        .then_inc(s_norm, 1)

                def gate_out(ch, r):
                    dve.wait_ge(o_done, (hg * 2 + ch) * 4 + r + 1)
                    own = NS + r * P
                    dve.tensor_tensor(res[:, bass.ds(hg * 2 + ch, 1), own:own + P].rearrange("p a n -> p (a n)"),
                                      DD[:, 0:P], zT[:, own:own + P], ALU.mult).then_inc(o_out, 1)

                for ch in range(2):
                    chunk = hg * 2 + ch
                    for g in range(NG):
                        v_out(ch, g)
                    largest(chunk, 0)
                    largest(chunk, 1)
                    normalise(chunk, 0)
                    normalise(chunk, 1)
                    for r in range(NCL):
                        if r < NCL - 1:
                            for u in (2 * r + 2, 2 * r + 3):
                                largest(chunk, u)
                                normalise(chunk, u)
                        gate_out(ch, r)

                dve.wait_ge(qkv_out, (hg + 1) * U_HG)
                for bh in range(2):
                    last = None
                    for ch in range(2):
                        for half in range(2):
                            rows, h = slice(HD * half, HD * half + HD), 2 * ch + half
                            src = lambda g: q_new[rows, g, ch, :].rearrange("p (q b) -> p b q", b=NB)[:, 4 * bh:4 * bh + 4, :]
                            to = lambda t: q_row[rows, bh, t, ch, :, h, :]
                            dve.tensor_copy(to(0), src(0))
                            dve.tensor_copy(to(TILES), src(1))
                            dve.tensor_copy(to(TILES + 1), src(2))
                            for r in range(4):
                                dve.tensor_copy(to(1 + r)[:, :, r::4], src(1)[:, :, r::4])
                            for r in range(8):
                                last = dve.tensor_copy(to(5 + r)[:, :, r:r + 1], src(2)[:, :, r:r + 1])
                    last.then_inc(q_rows, 1)
                for bh in range(2):
                    n = hg * 2 + bh + 1
                    S = pair[2 + bh]
                    dve.wait_ge(tile_used, RING + hg * TILES_HG + (bh + 1) * TILES)
                    dve.memset(neg_top[:, bh:bh + 1], 0.0)
                    dve.tensor_tensor_reduce(probs[:, bh, 0:SW], S[:, P:P + SW], mask_s[:, bh, :], 1.0, NEG, ALU.add,
                                             ALU.max, top[:, bh:bh + 1]).then_inc(ss_max, 1)
                    dve.wait_ge(ss_max, n)
                    dve.tensor_scalar(neg_top[:, bh:bh + 1], top[:, bh:bh + 1], -SCALE, None, ALU.mult).then_inc(ss_neg, 1)
                for bh in range(2):
                    n = hg * 2 + bh + 1
                    dve.wait_ge(ss_exp, n)
                    dve.reciprocal(share[:, bh:bh + 1], total[:, bh:bh + 1]).then_inc(ss_share, 1)
                    dve.wait_ge(ss_share, n)
                    dve.tensor_scalar(probs[:, bh, 0:SW], probs[:, bh, 0:SW], share[:, bh:bh + 1], None, ALU.mult)\
                        .then_inc(ss_norm, 1)
                for bh in range(2):
                    T, O = pair[bh], pair[2 + bh]
                    dve.wait_ge(spt_done, hg * 2 + bh + 1)
                    rows = lambda x: x.rearrange("p (m q) -> p m q", q=NQ)
                    dve.tensor_copy(p_new[:, :, :].rearrange("p g m -> p (g m)"), T[0:NS, 512:512 + NG * P])\
                        .then_inc(p_cols, 1)
                    dve.tensor_copy(p_col[:, 0, :], T[:, 0:P]).then_inc(p_cols, 1)
                    for r in range(4):
                        last = dve.tensor_copy(rows(p_col[:, 1 + r, :])[:, :, r::4], rows(T[:, P:2 * P])[:, :, r::4])
                    last.then_inc(p_cols, 1)
                    for r in range(8):
                        last = dve.tensor_copy(rows(p_col[:, 5 + r, :])[:, :, r:r + 1], rows(T[:, 2 * P:3 * P])[:, :, r:r + 1])
                    last.then_inc(p_cols, 2)
                    dve.wait_ge(tile_used, RING + hg * TILES_HG + (bh + 3) * TILES)
                    dve.tensor_tensor(o_own[:, :], O[:, 0:2 * P], head_mask[:, :], ALU.mult).then_inc(so_own, 1)
                    dve.wait_ge(sot_done, hg * 2 + bh + 1)
                    for ch in range(2):
                        cols = lambda x: x.rearrange("p (q b) -> p b q", b=NB)[:, 4 * bh:4 * bh + 4, :]
                        dve.tensor_tensor(cols(res[:, bass.ds(hg * 2 + ch, 1), 0:NS].rearrange("p a n -> p (a n)")),
                                          T[:, ch * 4 * NQ:(ch + 1) * 4 * NQ].rearrange("p (b q) -> p b q", b=4),
                                          cols(z_new[:, ch, :]), ALU.mult).then_inc(sot_out, 1)

            with dve.Fori(0, 2) as it:
                for m in range(4):
                    residual(it, m, N_OUT1, 1)
            norm(2)


def constants():
    i = np.arange(P)
    mask_p = np.full((P, NCL, PW), NEG, np.float32)
    for r in range(NCL):
        for c in range(NCL):
            back = 4 * (i[:, None] - i[None, :]) + r - c
            mask_p[:, r, c * P:(c + 1) * P][(back >= 0) & (back <= WIN[0])] = 0
        back = i[:, None] - i[None, :]
        mask_p[:, r, 4 * P:5 * P][back >= 0] = 0
        mask_p[:, r, 5 * P:6 * P][(back >= 0) & (back % 4 == 0)] = 0
    row = np.arange(P)
    b4, h, q = row // 32, row // 8 % 4, row % 8
    mask_s = np.zeros((P, 2, SW), np.float32)
    mask_s[:, :, 0:P][(i[None, :] < q[:, None])[:, None, :].repeat(2, 1)] = NEG
    mask_s[:, :, P:2 * P][(i[None, :] < q[:, None] // 4)[:, None, :].repeat(2, 1)] = NEG
    n = np.arange(NS)
    t, b = n // NB, n % NB
    for bh in range(2):
        same = b[None, :] == 4 * bh + b4[:, None]
        back = q[:, None] - t[None, :]
        for g in range(NG):
            ok = same & (back >= 0) & (back % DIL[g] == 0)
            mask_s[:, bh, NG * P + g * NS:NG * P + (g + 1) * NS][~ok] = NEG
    head_mask = (np.arange(2 * P)[None, :] // HD == h[:, None]).astype(np.float32)
    pick = np.zeros((P, 4 * NQ), np.float32)
    pick[row, b4 * NQ + q] = 1
    return dict(ident=np.eye(P, dtype=np.float32), mask_p=mask_p, mask_s=mask_s, head_mask=head_mask, pick=pick)


def units(*weights):
    return [np.ascontiguousarray(w.reshape(KC, P, P).transpose(1, 0, 2)).reshape(P, KC * P) for w in weights]


def kernel(**inputs):
    from concourse import bacc
    from concourse.bass_utils import run_bass_kernel_spmd

    x = {k: np.asarray(v) for k, v in inputs.items()}
    w0, w1 = x["conv_w_in"][0], x["attn_w_in"][0]
    cols = lambda w, at: w[:, at:at + P]
    order = [cols(w0, base + j * P) for j in range(KC) for base in (D, 0, 2 * D)]
    order += [cols(x["conv_w_out"][0], j * P) for j in range(KC)]
    order += [cols(w1, base * D + j * P) for j in range(KC) for base in range(U_CH)]
    order += [cols(x["attn_w_out"][0], j * P) for j in range(KC)]
    arrays = dict(constants())
    arrays["w_units"] = np.stack(units(*order))

    prompt = x["x_prompt"][0].reshape(P, NCL, D).transpose(1, 0, 2).reshape(SEQ, D)
    sample = x["x_sample"].transpose(1, 0, 2).reshape(NS, D)
    chunks = lambda a: np.ascontiguousarray(a.reshape(a.shape[0], KC, P).transpose(2, 1, 0))
    arrays["xT"] = chunks(np.concatenate([sample, prompt]))
    arrays["vec"] = chunks(np.concatenate([x["conv_dw_w"][0], x["conv_dw_b"], x["conv_ln_g"], x["conv_ln_b"],
                                           x["norm_g"][0:1], x["norm_b"][0:1], x["norm_g"][1:2], x["norm_b"][1:2],
                                           np.full((1, D), EPS, np.float32)]))
    arrays["state"] = chunks(x["state_conv"][0].transpose(1, 0, 2).reshape(HALO * NB, D))
    k_tiles, v_tiles = [], []
    caches = [x[f"cache_kv_w{w}_d{dil}"][0] for w, dil in zip(WIN, DIL)]
    for g, c in enumerate(caches):
        arrays[f"cache{g}"] = c.reshape(NB, WIN[g] * 2 * D)
        c = c.reshape(2, 4, P, DIL[g], 2, HG, 2 * P)[:, :, :, 0:8]
        k_tiles.append(c[:, :, :, :, 0].reshape(2, 4, P, -1, HG, 2, P).transpose(4, 0, 3, 6, 5, 1, 2))
        v_tiles.append(c[:, :, :, :, 1].transpose(4, 0, 3, 2, 1, 5))
    arrays["k_tiles"] = np.concatenate([a.reshape(HG, 2, -1, P, 2 * 4 * P) for a in k_tiles], 2).reshape(-1, P, 2 * 4 * P)
    arrays["v_tiles"] = np.concatenate([a.reshape(HG, 2, -1, P, 2 * 4 * P) for a in v_tiles], 2).reshape(-1, P, 2 * 4 * P)

    nc = bacc.Bacc("TRN2", target_bir_lowering=False, num_devices=1)
    d = {n: nc.dram_tensor(n, a.shape, F32, kind="ExternalInput").ap() for n, a in arrays.items()}
    shapes = dict(yT=(P, KC, NT), kv_new=(KC * NG * 2, P, NT), conv_p=(P, KC, HALO), conv_s=(P, KC, HALO * NB),
                  **{f"kept{g}": (NB, (WIN[g] - NQ) * 2 * D) for g in range(NG)})
    o = {n: nc.dram_tensor(n, s, F32, kind="ExternalOutput").ap() for n, s in shapes.items()}
    build(nc, d, o)
    got = run_bass_kernel_spmd(nc, [arrays], core_ids=[0]).results[0]

    def tokens(a):
        a = np.moveaxis(a, -1, -2)
        s, p = a[..., :NS, :], a[..., NS:, :]
        p = np.swapaxes(p.reshape(*a.shape[:-2], NCL, P, D), -3, -2).reshape(*a.shape[:-2], SEQ, D)
        return p, np.swapaxes(s.reshape(*a.shape[:-2], NQ, NB, D), -3, -2)

    yp, ys = tokens(got["yT"].transpose(1, 0, 2).reshape(D, NT))
    kv = got["kv_new"].reshape(KC, NG, 2, P, NT).transpose(1, 2, 0, 3, 4).reshape(NG, 2, D, NT)
    kvp, kvs = tokens(kv)
    heads = lambda a: a.reshape(*a.shape[:-1], D // HD, HD)
    out_p, out_s = [], []
    for g in range(NG):
        keep = min(WIN[g], SEQ)
        out_p.append(heads(kvp[g].transpose(1, 0, 2))[None, None, -keep:])
        new = heads(kvs[g].transpose(1, 2, 0, 3))
        out_s.append(np.concatenate([got[f"kept{g}"].reshape(NB, WIN[g] - NQ, 2, D // HD, HD), new], 1)[None])
    conv_p = got["conv_p"].transpose(2, 1, 0).reshape(1, 1, HALO, D)
    conv_s = got["conv_s"].transpose(2, 1, 0).reshape(HALO, NB, D).transpose(1, 0, 2)[None]
    c = np.ascontiguousarray
    return (c(yp[None]), c(ys), *map(c, out_p), c(conv_p), *map(c, out_s), c(conv_s))
```

```python
from contextlib import ExitStack

import concourse.bass as bass
from concourse import mybir
import numpy as np

F32 = mybir.dt.float32
F32R = mybir.dt.float32r
ALU = mybir.AluOpType
ACT = mybir.ActivationFunctionType

P = 128
D = 1024
KC = D // P
SEQ = 512
NB = 8
NQ = 8
NS = NB * NQ
NT = NS + SEQ
NCL = 4
W = 31
HALO = W - 1
HD = 64
NG = 3
WIN = (128, 512, 2048)
DIL = (1, 4, 16)
HG = 4
TILES = 1 + 4 + 8
GROUP_OF = [0] + [1] * 4 + [2] * 8
FIRST_OF = (0, 1, 5)
SCALE = HD ** -0.5
ALPHA = 4.0 ** 0.25
EPS = 1e-5
NEG = -1e30

U_IN0 = 3 * KC
U_OUT0 = KC
KINDS = [("q", 0), ("k", 0), ("v", 0), ("z", 0), ("q", 1), ("k", 1), ("v", 1), ("q", 2), ("k", 2), ("v", 2)]
U_CH = len(KINDS)
U_HG = 2 * U_CH
N_OUT0 = U_IN0
N_IN1 = U_IN0 + U_OUT0
N_OUT1 = N_IN1 + HG * U_HG
UNITS = N_OUT1 + KC
LAND = 4
RING = 5
TILES_HG = 4 * TILES
STEPS = (3, 3, 3, 2, 2) + (4, 3, 3, 3, 0) + (0, 4, 3, 3, 3) + (4, 3, 3, 3, 0)
TAIL_AT = (0, 7, 13, 19, 26, 26, 32, 39, 42)
TAIL_LOADS = (8, 14, 20, 26)
SAMPLE_STEPS = 8 + KC
STEP_AT = [sum(STEPS[:m]) for m in range(U_HG + 1)]

T0 = 512 - NS - 2 * P
SPLIT = NS + 2 * P
V_DWB, V_LNG, V_LNB, V_G0, V_B0, V_G1, V_B1, V_EPS = range(W, W + 8)
NV = W + 8

SW = NG * P + NG * NS
PW = NCL * P + 2 * P
COPY_ROWS = (120, 252, 255)
COPY_RUNS = (16, 32, 32)
UW = HALO + SEQ + (HALO + NQ) * NB
US = HALO + SEQ

ACT_TAPS = 8
DVE_TAPS = W - ACT_TAPS


def build(nc, d, o):
    with ExitStack() as ctx:
        def sb(name, shape, dt=F32, where=ctx):
            return where.enter_context(nc.sbuf_tensor(name, shape, dt))

        def sem(name):
            return ctx.enter_context(nc.semaphore(name))

        act_hi = sb("act_hi", [P, KC, NT], F32R)
        act_lo = sb("act_lo", [P, KC, NT], F32R)
        res = sb("res", [P, KC, NT])
        landing = sb("landing", [P, LAND, KC * P])
        w_hi = sb("w_hi", [P, 2, KC * P], F32R)
        w_lo = sb("w_lo", [P, 2, KC * P], F32R)
        ident = sb("ident_sb", [P, P])
        ones = sb("ones", [P, P])
        vec = sb("vec_sb", [P, KC, NV])
        mask_p = sb("mask_p_sb", [P, NCL, PW])
        mask_s = sb("mask_s_sb", [P, 2, SW])
        head_mask = sb("head_mask_sb", [P, 2 * P])
        pick = sb("pick_sb", [P, 4 * NQ])

        with ExitStack() as lay0:
            with ExitStack() as early:
                u_in = sb("u_in", [P, KC, UW], where=early)
                prod = sb("prod", [P, W, NS], where=early)
            mid_hi = sb("mid_hi", [P, KC, NT], F32R, where=lay0)
            mid_lo = sb("mid_lo", [P, KC, NT], F32R, where=lay0)
            zs = sb("zs", [P, KC, NT], where=lay0)
            sg = sb("sg", [P, 2, NT], where=lay0)
            neg_mean = sb("neg_mean", [P, NT], where=lay0)
            std = sb("std", [P, NT], where=lay0)
            rstd = sb("rstd", [P, NT], where=lay0)
            sq = sb("sq", [P, 2, NT], where=lay0)
            odd_sum = sb("odd_sum", [P, 2, SEQ], where=lay0)
            pool_sum = sb("pool_sum", [P, 2, SEQ], where=lay0)
            tap_prod = sb("tap_prod", [P, ACT_TAPS - 1, SEQ], where=lay0)
        with ExitStack() as tail:
            mid1_hi = sb("mid1_hi", [P, KC, SEQ], F32R, where=tail)
            mid1_lo = sb("mid1_lo", [P, KC, SEQ], F32R, where=tail)
            ys = sb("ys", [P, KC, NS], where=tail)
            ys_sq = sb("ys_sq", [P, KC, NS], where=tail)
            neg_mean1 = sb("neg_mean1", [P, SEQ], where=tail)
            std1 = sb("std1", [P, SEQ], where=tail)
            rstd1 = sb("rstd1", [P, SEQ], where=tail)
            sq1 = sb("sq1", [P, 2, SEQ], where=tail)
        with ExitStack() as lay1:
            qT = sb("qT", [P, NG, NT], where=lay1)
            kT = sb("kT", [P, NG, NT], where=lay1)
            vT = sb("vT", [P, 2, NT], where=lay1)
            v_nat = sb("v_nat", [P, NG, NCL, P], where=lay1)
            zT = sb("zT", [P, NT], where=lay1)
            probs = sb("probs", [P, 2, PW], where=lay1)
            probsT = sb("probsT", [P, 2, PW], where=lay1)
            q_new = sb("q_new", [P, NG, 2, NS], where=lay1)
            k_new = sb("k_new", [P, NG, 2, NS], where=lay1)
            v_new = sb("v_new", [NS, NG, 2 * P], where=lay1)
            z_new = sb("z_new", [P, 2, NS], where=lay1)
            q_old = sb("q_old", [P, NG, 2, NS], where=lay1)
            k_old = sb("k_old", [P, NG, 2, NS], where=lay1)
            v_old = sb("v_old", [NS, NG, 2 * P], where=lay1)
            z_old = sb("z_old", [P, 2, NS], where=lay1)
            ring = sb("ring", [P, RING, 2 * 4 * P], where=lay1)
            q_row = sb("q_row", [P, TILES + 2, 2, 4, 4, NQ], where=lay1)
            s_probs = sb("s_probs", [P, 2, SW], where=lay1)
            p_col = sb("p_col", [P, TILES, P], where=lay1)
            p_new = sb("p_new", [NS, NG, P], where=lay1)
            o_own = sb("o_own", [P, 2 * P], where=lay1)
            neg_top = sb("neg_top", [P, 2], where=lay1)
            total = sb("total", [P, 2], where=lay1)
            share = sb("share", [P, 2], where=lay1)
            s_neg_top = sb("s_neg_top", [P, 2], where=lay1)
            s_total = sb("s_total", [P, 2], where=lay1)
            s_part = sb("s_part", [P, 2], where=lay1)

        pair = [ctx.enter_context(nc.psum_tensor(f"pair{x}", [P, 1024], F32)) for x in "ABCD"]
        A, B, C, DD = pair

        consts_in = [sem(f"consts_in{i}") for i in range(6)]
        x_in = [sem(f"x_in{h}") for h in range(4)]
        state_in = sem("state_in")
        w_landed = [sem(f"w_landed{s}") for s in range(LAND)]
        w_split = sem("w_split")
        hi_done = sem("hi_done")
        proj_done = sem("proj_done")
        x_hi = sem("x_hi")
        x_split = sem("x_split")
        y_split = [sem("y_split_pool"), sem("y_split_dve")]
        made = sem("made")
        gate_done = sem("gate_done")
        z_done = sem("z_done")
        silu_done = sem("silu_done")
        u_done = sem("u_done")
        prod_done = sem("prod_done")
        conv = sem("conv")
        tap_done = sem("tap_done")
        tap_added = sem("tap_added")
        conv_merged = sem("conv_merged")
        sconv = sem("sconv")
        ln_sum = sem("ln_sum")
        ln_mean = sem("ln_mean")
        ln_cent = sem("ln_cent")
        ln_sq = sem("ln_sq")
        ln_sqsum = sem("ln_sqsum")
        ln_std = sem("ln_std")
        ln_rstd = sem("ln_rstd")
        ln_scaled = sem("ln_scaled")
        ln_act = sem("ln_act")
        gated = sem("gated")
        mid1_hi_done = sem("mid1_hi_done")
        mid1_split = [sem("mid1_split_pool"), sem("mid1_split_dve")]
        sample_out = sem("sample_out")
        mid_hi_done = sem("mid_hi_done")
        mid_split = sem("mid_split")
        res_part = sem("res_part")
        res_done = sem("res_done")
        qkv_out = sem("qkv_out")
        vt_done = sem("vt_done")
        v_ready = sem("v_ready")
        s_done = sem("s_done")
        s_max = sem("s_max")
        s_exp = sem("s_exp")
        s_share = sem("s_share")
        s_norm = sem("s_norm")
        pt_done = sem("pt_done")
        pt_out = sem("pt_out")
        o_done = sem("o_done")
        o_out = sem("o_out")
        rows_cleared = sem("rows_cleared")
        handed = sem("handed")
        handing = sem("handing")
        q_rows = sem("q_rows")
        tile_in = [sem(f"tile_in{s}") for s in range(RING)]
        tile_used = sem("tile_used")
        ss_max = sem("ss_max")
        ss_exp = sem("ss_exp")
        ss_share = sem("ss_share")
        ss_norm = sem("ss_norm")
        spt_done = sem("spt_done")
        p_cols = sem("p_cols")
        so_own = sem("so_own")
        sot_done = sem("sot_done")
        sot_out = sem("sot_out")
        k_stored = [sem(f"k_stored{g}") for g in range(NG)]
        v_stored = [sem(f"v_stored{s}") for s in range(2)]
        u_stored = sem("u_stored")
        y_stored = sem("y_stored")
        copied = sem("copied")

        block = ctx.enter_context(nc.Block())

        def score_pair(ch, u):
            return pair[2 + ch] if u == 0 else A if u == 1 else pair[u % 2]

        def tok(x, lo=0, hi=NT):
            return pair[x][:, T0 + lo:T0 + hi]

        @block.sync
        def _(sp):
            def load_unit(n, slot):
                sp.wait_ge(w_split, n + 1)
                sp.dma_start(landing[:, slot, :], d["w_units"][bass.ds(n, 1)].rearrange("a p m -> (a p) m"))\
                    .then_inc(w_landed[slot], 16)

            def copy_rows(g, b, piece):
                n = COPY_ROWS[g] * 2 * D
                src = d[f"cache{g}"][bass.ds(b, 1), (piece * n + NQ * 2 * D):(piece * n + NQ * 2 * D + n)]
                dst = o[f"kept{g}"][bass.ds(b, 1), piece * n:piece * n + n]
                sp.dma_start(dst.rearrange("a (r m) -> (a r) m", r=COPY_RUNS[g]),
                             src.rearrange("a (r m) -> (a r) m", r=COPY_RUNS[g])).then_inc(copied, 16)

            def store_u(j):
                sp.wait_ge(u_done, 2 * j + 4)
                sp.wait_ge(state_in, 16)
                sp.dma_start(o["conv_p"][:, j, :], u_in[:, j, SEQ:SEQ + HALO]).then_inc(u_stored, 16)
                sp.dma_start(o["conv_s"][:, j, :], u_in[:, j, US + NQ * NB:UW]).then_inc(u_stored, 16)

            def load_x(h):
                sp.dma_start(res[:, 2 * h:2 * h + 2, :], d["xT"][:, 2 * h:2 * h + 2, :]).then_inc(x_in[h], 16)

            def load_first(n):
                sp.dma_start(landing[:, n, :], d["w_units"][n]).then_inc(w_landed[n], 16)

            def load_const(i, dst, name):
                sp.dma_start(dst, d[name]).then_inc(consts_in[i], 16)

            load_first(0)
            for h in range(4):
                load_x(h)
                if h == 1:
                    load_first(1)
            load_const(0, vec[:, :, :], "vec")
            load_first(2)
            load_first(3)
            sp.wait_ge(made, 6)
            sp.dma_start(u_in[:, :, US:US + HALO * NB], d["state"]).then_inc(state_in, 16)
            for i, (dst, name) in enumerate(((ident[:, :], "ident"), (mask_p[:, :, :], "mask_p"),
                                             (mask_s[:, :, :], "mask_s"), (head_mask[:, :], "head_mask"),
                                             (pick[:, :], "pick"))):
                load_const(i + 1, dst, name)

            for j in range(KC):
                for i in range(3):
                    load_unit(3 * j + i + LAND, (3 * j + i) % LAND)
                    copy_rows(2, j, i)
                if j:
                    store_u(j - 1)
            store_u(KC - 1)
            for b in range(NB):
                copy_rows(1, b, 0)
            with sp.Fori(0, 2) as it:
                for m in range(4):
                    load_unit(N_OUT0 + it * 4 + m + LAND, m)
                    copy_rows(2, it * 4 + m, 3)

            for ch in range(2):
                for piece in (6, 7):
                    copy_rows(2, ch, piece)

            def load_tile(hg, t):
                last = t - RING if t >= RING else t - TILES_HG + (TILES_HG - 1 - t) // RING * RING
                sp.wait_ge(tile_used, RING + hg * TILES_HG + last + 1)
                which, tt = divmod(t, TILES)
                if which == 4:
                    sp.dma_start(ring[:, t % RING, :], d["w_units"][N_OUT1 + tt]).then_inc(tile_in[t % RING], 16)
                    return
                src = d["k_tiles" if which < 2 else "v_tiles"]
                sp.dma_start(ring[:, t % RING, :],
                             src[bass.ds((hg * 2 + which % 2) * TILES + tt, 1)].rearrange("a p m -> (a p) m"))\
                    .then_inc(tile_in[t % RING], 16)

            def store_kv(hg, m):
                ch, i = divmod(m, U_CH)
                kind, g = KINDS[i]
                if kind not in "kv":
                    return
                sp.wait_ge(qkv_out, hg * U_HG + m + 1)
                sp.dma_start(o["kv_new"][bass.ds((hg * 2 + ch) * 6 + g * 2 + "kv".index(kind), 1)]
                             .rearrange("a p n -> (a p) n"), kT[:, g, :] if kind == "k" else vT[:, g % 2, :])\
                    .then_inc(k_stored[g] if kind == "k" else v_stored[g % 2], 16)

            def load_group(hg, first):
                for m in range(U_HG):
                    ch, i = divmod(m, U_CH)
                    load_unit(N_IN1 + hg * U_HG + m + LAND, m % LAND)
                    if i:
                        store_kv(hg, m - 1)
                    if not first:
                        for t in range(STEP_AT[m], STEP_AT[m + 1]):
                            load_tile(hg - 1, t)
                    if i == U_CH - 1:
                        copy_rows(0, hg * 2 + ch, 0)
                        copy_rows(1, hg * 2 + ch, 1)
                    if first and i >= 2:
                        copy_rows(2, i - 2, 4 + ch)
                    if not first and i >= U_CH - 2:
                        copy_rows(2, hg * 2 + ch, 6 + i - (U_CH - 2))
                    if i == U_CH - 1:
                        store_kv(hg, m)

            load_group(0, True)
            with sp.Fori(1, HG) as hg:
                load_group(hg, False)
            for t in range(TILES_HG + LAND):
                load_tile(HG - 1, t)
                if t in TAIL_LOADS:
                    n = N_OUT1 + LAND + TAIL_LOADS.index(t)
                    load_unit(n, n % LAND)
            for k in range(KC):
                sp.wait_ge(ln_act, 2 * KC + k + 1)
                sp.dma_start(o["yT"][:, k, NS:NT], res[:, k, NS:NT]).then_inc(y_stored, 16)
            sp.wait_ge(sample_out, SAMPLE_STEPS)
            sp.dma_start(o["yT"][:, :, 0:NS], ys[:, :, :]).then_inc(y_stored, 16)
            sp.wait_ge(copied, 16 * NB * (1 + 2 + 8))
            for g in range(NG):
                sp.wait_ge(k_stored[g], 16 + 16 * KC)
            sp.wait_ge(v_stored[0], 16 + 16 * 2 * KC)
            sp.wait_ge(v_stored[1], 16 + 16 * KC)
            sp.wait_ge(u_stored, 16 * 2 * KC)
            sp.wait_ge(y_stored, 16 * (KC + 1))

        @block.tensor
        def _(pe):
            def unit(n, s, src_hi, src_lo, parts=None):
                pe.wait_ge(w_split, LAND + n + 1)
                for k in range(KC):
                    if parts is not None:
                        parts(k)
                    for q, (w, x) in enumerate(((w_hi, src_hi), (w_hi, src_lo), (w_lo, src_hi))):
                        first, last = k == 0 and q == 0, k == KC - 1 and q == 2
                        lhs = w[:, s, k * P:(k + 1) * P]
                        pe.matmul(tok(s, 0, SPLIT), lhs, x[:, k, 0:SPLIT], start=first, stop=last)
                        mm = pe.matmul(tok(s, SPLIT, NT), lhs, x[:, k, SPLIT:NT], start=first, stop=last)
                mm.then_inc(proj_done, 1)

            def norm_sum(round_, k):
                if round_ == 0:
                    pe.wait_ge(conv_merged, 4 + 2 * (k + 1))
                    pe.wait_ge(sconv, 2 * (k + 1))
                else:
                    pe.wait_ge(res_done, KC * (round_ - 1) + k + 1)
                pe.matmul(tok(2, 0, SPLIT), ones[:, :], res[:, k, 0:SPLIT], start=k == 0, stop=k == KC - 1)
                mm = pe.matmul(tok(2, SPLIT, NT), ones[:, :], res[:, k, SPLIT:NT], start=k == 0, stop=k == KC - 1)
                if k == KC - 1:
                    mm.then_inc(ln_sum, 1)

            def norm_squares(round_):
                for k in range(KC):
                    pe.wait_ge(ln_sq, KC * round_ + k + 1)
                    pe.matmul(tok(3, 0, SPLIT), ones[:, :], sq[:, k % 2, 0:SPLIT], start=k == 0, stop=k == KC - 1)
                    pe.matmul(tok(3, SPLIT, NT), ones[:, :], sq[:, k % 2, SPLIT:NT], start=k == 0,
                              stop=k == KC - 1).then_inc(ln_sqsum, 1)

            def out_projection(base, round_, parts):
                for m in range(KC):
                    pe.wait_ge(res_part, KC * round_ + m + 1)
                    unit(base + m, m % 2, mid_hi, mid_lo, parts if m == 0 else None)
                    if m:
                        norm_sum(round_ + 1, m - 1)
                norm_sum(round_ + 1, KC - 1)
                norm_squares(round_ + 1)

            pe.wait_ge(made, 6)
            with pe.Fori(0, 2) as it:
                for jj in range(4):
                    for i in range(3):
                        if i == 0:
                            pe.wait_ge(u_done, (it * 4 + jj) * 2 + 2)
                        elif i == 1:
                            pe.wait_ge(z_done, it * 4 + jj + 1)
                        else:
                            pe.wait_ge(gate_done, it * 4 + jj + 1)
                        unit(it * 12 + 3 * jj + i, (3 * jj + i) % 2, act_hi, act_lo,
                             (lambda k: pe.wait_ge(x_split, k + 1)) if i == jj == 0 else None)
            for k in range(KC):
                norm_sum(0, k)
            norm_squares(0)
            pe.wait_ge(z_done, 1 + KC)
            out_projection(N_OUT0, 0, lambda k: pe.wait_ge(mid_split, k + 1))
            for i in range(1, 6):
                pe.wait_ge(consts_in[i], 16)

            def tile_ready(hg, t):
                slot, uses = t % RING, (TILES_HG - t % RING + RING - 1) // RING
                pe.wait_ge(tile_in[slot], (hg * uses + t // RING + 1) * 16)

            def score_rows(t, S, cols, first, last, keys):
                for ch in range(2):
                    for b in range(4):
                        mm = pe.matmul(S[32 * b:32 * b + 32, cols],
                                       q_row[:, t, ch, b, :, :].rearrange("p h q -> p (h q)"),
                                       keys(ch, b), start=first and ch == 0, stop=last and ch == 1)
                return mm

            def key_tiles(hg, bh, lo_, hi_):
                S = pair[2 + bh]
                if lo_ == 0:
                    pe.wait_ge(o_out, (hg + 1) * 8)
                for t in range(lo_, hi_):
                    tt = bh * TILES + t
                    g = GROUP_OF[t]
                    if t in FIRST_OF:
                        pe.wait_ge(q_rows, (hg * 2 + bh) * NG + g + 1)
                        score_rows((0, TILES, TILES + 1)[g], S, slice(512 + g * NS, 512 + (g + 1) * NS), True, True,
                                   lambda ch, b: k_old[:, g, ch, :])
                    tile_ready(hg, tt)
                    kt = ring[:, tt % RING, :].rearrange("p (c b n) -> p c b n", c=2, b=4)
                    score_rows(t, S, slice(P + g * P, P + (g + 1) * P), t in FIRST_OF, t + 1 in FIRST_OF + (TILES,),
                               lambda ch, b: kt[:, ch, b, :]).then_inc(tile_used, 1)

            def turn_rows(hg, bh, T):
                pe.wait_ge(ss_norm, hg * 2 + bh + 1)
                for g in range(NG):
                    pe.transpose(T[:, g * P:(g + 1) * P], s_probs[:, bh, g * P:(g + 1) * P], ident[:, :])
                for g in range(NG):
                    mm = pe.transpose(T[0:NS, 512 + g * P:512 + (g + 1) * P],
                                      s_probs[:, bh, NG * P + g * NS:NG * P + (g + 1) * NS], ident[:, :])
                mm.then_inc(spt_done, 1)

            def value_tiles(hg, bh, lo_, hi_):
                if lo_ == 0 and bh:
                    pe.wait_ge(so_own, hg * 2 + 1)
                for t in range(lo_, hi_):
                    tt = (2 + bh) * TILES + t
                    if t in FIRST_OF:
                        pe.wait_ge(p_cols, (hg * 2 + bh) * (1 + NG) + 2 + GROUP_OF[t])
                    tile_ready(hg, tt)
                    for b in range(4):
                        mm = pe.matmul(C[32 * b:32 * b + 32, 0:2 * P], p_col[:, t, 32 * b:32 * b + 32],
                                       ring[:, tt % RING, b * 2 * P:(b + 1) * 2 * P],
                                       start=t == 0, stop=t == TILES - 1)
                    mm.then_inc(tile_used, 1)
                    for g in range(NG if t == 0 else 0):
                        for b in range(4):
                            pe.matmul(C[32 * b:32 * b + 32, 0:2 * P], p_new[:, g, 32 * b:32 * b + 32],
                                      v_old[:, g, :], start=False, stop=False)

            def rows_to_columns(hg, bh):
                pe.wait_ge(so_own, hg * 2 + bh + 1)
                if bh:
                    pe.wait_ge(sot_out, hg * 4 + 2)
                for ch in range(2):
                    mm = pe.matmul(C[:, 512 + ch * 4 * NQ:512 + (ch + 1) * 4 * NQ], o_own[:, ch * P:(ch + 1) * P],
                                   pick[:, :], start=True, stop=True)
                mm.then_inc(sot_done, 1)

            def mix(chunk, r):
                pe.wait_ge(pt_out, chunk * 8 + 2 * r + 2)
                if r:
                    pe.wait_ge(o_out, chunk * 4 + r)
                else:
                    pe.wait_ge(v_ready, chunk * 6 + 6)
                for c in range(6):
                    v = v_nat[:, 0, c, :] if c < 4 else v_nat[:, c - 3, r, :]
                    for h in range(2):
                        mm = pe.matmul(DD[HD * h:HD * h + HD, 0:P], v[:, HD * h:HD * h + HD],
                                       probsT[:, h, c * P:(c + 1) * P], start=c == 0, stop=c == 5)
                mm.then_inc(o_done, 1)

            def group(hg, first):
                def v_turn(ch, g, V):
                    pe.wait_ge(qkv_out, hg * U_HG + ch * U_CH + KINDS.index(("v", g)) + 1)
                    for c in range(NCL):
                        pe.transpose(V[:, c * P:(c + 1) * P], vT[:, g % 2, NS + c * P:NS + (c + 1) * P], ident[:, :])
                    pe.transpose(V[0:NS, 512:512 + P], vT[:, g % 2, 0:NS], ident[:, :]).then_inc(vt_done, 1)

                def scores(ch, u):
                    r, h = divmod(u, 2)
                    rows = slice(HD * h, HD * h + HD)
                    own = slice(NS + r * P, NS + (r + 1) * P)
                    S = score_pair(ch, u)
                    if u == 0:
                        pe.wait_ge(qkv_out, hg * U_HG + ch * U_CH + 9)
                        if not first:
                            pe.wait_ge(*((p_cols, hg * 2 * (1 + NG)) if ch else (ss_max, hg * 2 - 1)))
                    elif u == 3:
                        pe.wait_ge(qkv_out, hg * U_HG + (ch + 1) * U_CH)
                    elif u > 1:
                        pe.wait_ge(s_max, (hg * 2 + ch) * 8 + max(u - 1, 2))
                    pe.matmul(S[:, 0:512], qT[rows, 0, own], kT[rows, 0, NS:NT], start=True, stop=True)
                    pe.matmul(S[:, 512:640], qT[rows, 1, own], kT[rows, 1, own], start=True, stop=True)
                    pe.matmul(S[:, 640:768], qT[rows, 2, own], kT[rows, 2, own], start=True, stop=True)\
                        .then_inc(s_done, 1)

                def turn_probs(ch, u):
                    su = (hg * 2 + ch) * 8 + u
                    pe.wait_ge(s_norm, su + 1)
                    if ch or u:
                        pe.wait_ge(pt_out, su)
                    for c in range(6):
                        mm = pe.transpose(C[:, c * P:(c + 1) * P], probs[:, u % 2, c * P:(c + 1) * P], ident[:, :])
                    mm.then_inc(pt_done, 1)

                for ch in range(2):
                    for i in range(U_CH):
                        m = ch * U_CH + i
                        if i >= 2:
                            pe.wait_ge(qkv_out, hg * U_HG + m - 1)
                        if i in (4, 8):
                            pe.wait_ge(v_ready, (hg * 2 + ch) * 6 + i // 2)
                        unit(N_IN1 + hg * U_HG + m, m % 2, act_hi, act_lo,
                             (lambda k: pe.wait_ge(y_split[k % 2], k // 2 + 1)) if first and m == 0 else None)
                        if i == 0 and not (first and ch == 0):
                            mix(hg * 2 + ch - 1, NCL - 1)
                        if i in (3, 7):
                            v_turn(ch, i // 4, A)
                        if first:
                            pass
                        elif ch == 0:
                            bh = i // 5
                            key_tiles(hg - 1, bh, STEP_AT[m] - bh * TILES, STEP_AT[m + 1] - bh * TILES)
                        else:
                            bh = i // 5
                            if i == 5:
                                rows_to_columns(hg - 1, 0)
                            if STEPS[m]:
                                value_tiles(hg - 1, bh, STEP_AT[m] - (2 + bh) * TILES, STEP_AT[m + 1] - (2 + bh) * TILES)
                            if i == 0:
                                pe.wait_ge(o_out, hg * 8 + 4)
                                turn_rows(hg - 1, 0, DD)
                            if i == 4:
                                turn_rows(hg - 1, 1, DD)
                        if i == 8:
                            scores(ch, 0)
                            scores(ch, 1)
                    if ch and not first:
                        rows_to_columns(hg - 1, 1)
                    scores(ch, 2)
                    if ch and not first:
                        pe.wait_ge(sot_out, hg * 4)
                    turn_probs(ch, 0)
                    if ch == 0 and not first:
                        pe.wait_ge(ss_max, hg * 2)
                    v_turn(ch, 2, DD)
                    turn_probs(ch, 1)
                    scores(ch, 3)
                    mix(hg * 2 + ch, 0)
                    for r in range(1, NCL - 1):
                        turn_probs(ch, 2 * r)
                        scores(ch, 2 * r + 2)
                        turn_probs(ch, 2 * r + 1)
                        scores(ch, 2 * r + 3)
                        mix(hg * 2 + ch, r)
                    turn_probs(ch, 2 * NCL - 2)
                    turn_probs(ch, 2 * NCL - 1)

            group(0, True)
            with pe.Fori(1, HG) as hg:
                group(hg, False)
            mix(KC - 1, NCL - 1)

            hg = HG - 1

            def tiles(lo_, hi_):
                for which in range(4):
                    at = [min(max(t - which * TILES, 0), TILES) for t in (lo_, hi_)]
                    if at[0] < at[1]:
                        (key_tiles if which < 2 else value_tiles)(hg, which % 2, *at)

            def prompt_unit(m):
                n, s = N_OUT1 + m, m % 2
                pe.wait_ge(w_split, LAND + n + 1)
                pe.wait_ge(res_part, KC + m + 1)
                for k in range(KC):
                    if m == 0:
                        pe.wait_ge(mid1_split[k % 2], k // 2 + 1)
                    for q, (w, x) in enumerate(((w_hi, mid1_hi), (w_hi, mid1_lo), (w_lo, mid1_hi))):
                        mm = pe.matmul(pair[s][:, 0:SEQ], w[:, s, k * P:(k + 1) * P], x[:, k, :],
                                       start=k == 0 and q == 0, stop=k == KC - 1 and q == 2)
                mm.then_inc(proj_done, 1)

            def prompt_sum(k):
                pe.wait_ge(res_done, KC + k + 1)
                mm = pe.matmul(A[:, 512:512 + SEQ], ones[:, :], res[:, k, NS:NT], start=k == 0, stop=k == KC - 1)
                if k == KC - 1:
                    mm.then_inc(ln_sum, 1)

            def prompt_squares(lo_, hi_):
                for k in range(lo_, hi_):
                    pe.wait_ge(ln_sq, 2 * KC + k + 1)
                    pe.matmul(B[:, 512:512 + SEQ], ones[:, :], sq1[:, k % 2, :], start=k == 0, stop=k == KC - 1)\
                        .then_inc(ln_sqsum, 1)

            tiles(0, TAIL_AT[1])
            for m in range(KC):
                prompt_unit(m)
                if m:
                    prompt_sum(m - 1)
                if m < KC - 1:
                    tiles(TAIL_AT[m + 1], TAIL_AT[m + 2])
                if m == 3:
                    pe.wait_ge(ss_max, HG * 2)
                    turn_rows(hg, 0, DD)
                if m == 5:
                    pe.wait_ge(p_cols, (hg * 2 + 1) * (1 + NG))
                    turn_rows(hg, 1, DD)
                if m == 6:
                    rows_to_columns(hg, 0)
            tiles(TAIL_AT[KC], 45)
            prompt_sum(KC - 1)
            tiles(45, 48)
            prompt_squares(0, 4)
            tiles(48, 50)
            prompt_squares(4, KC)
            tiles(50, TILES_HG)
            rows_to_columns(hg, 1)

            pe.wait_ge(sot_out, HG * 4)
            for m in (*range(LAND, KC), *range(LAND)):
                if m < LAND:
                    tile_ready(hg, TILES_HG + m)
                w = landing[:, m % LAND, :] if m >= LAND else ring[:, (TILES_HG + m) % RING, :]
                for k in range(KC):
                    mm = pe.matmul(DD[:, m * NS:(m + 1) * NS], w[:, k * P:(k + 1) * P], res[:, k, 0:NS],
                                   start=k == 0, stop=k == KC - 1)
            mm.then_inc(proj_done, 1)
            pe.wait_ge(sample_out, 2)
            for k in range(KC):
                mm = pe.matmul(C[:, 0:NS], ones[:, :], ys[:, k, :], start=k == 0, stop=k == KC - 1)
            mm.then_inc(ln_sum, 1)
            pe.wait_ge(sample_out, 5)
            for k in range(KC):
                mm = pe.matmul(C[:, 512:512 + NS], ones[:, :], ys_sq[:, k, :], start=k == 0, stop=k == KC - 1)
            mm.then_inc(ln_sqsum, 1)

        @block.scalar
        def _(act):
            def split_hi(base, it, per, m):
                n = base + it * per + m
                act.wait_ge(w_landed[m % LAND], (base // LAND + it * (per // LAND) + m // LAND + 1) * 16)
                if m >= 2:
                    act.wait_ge(proj_done, n - 1)
                act.activation(w_hi[:, m % 2, :], landing[:, m % LAND, :], ACT.Copy).then_inc(hi_done, 1)

            def norm(round_):
                act.wait_ge(ln_sum, round_ + 1)
                act.activation(neg_mean[:, :], tok(2), ACT.Copy, scale=-1.0 / D).then_inc(ln_mean, 1)
                for k in range(KC):
                    act.wait_ge(ln_cent, KC * round_ + k + 1)
                    if k >= 2:
                        act.wait_ge(ln_sqsum, KC * round_ + k - 1)
                    act.activation(sq[:, k % 2, :], res[:, k, :], ACT.Square).then_inc(ln_sq, 1)
                act.wait_ge(ln_sqsum, KC * (round_ + 1))
                act.activation(std[:, :], tok(3), ACT.Sqrt, scale=1.0 / D, bias=vec[:, 0, V_EPS:V_EPS + 1]).then_inc(ln_std, 1)

            split_hi(0, 0, 0, 0)
            for k in range(KC):
                if k % 2 == 0:
                    act.wait_ge(x_in[k // 2], 16)
                act.activation(act_hi[:, k, :], res[:, k, :], ACT.Copy).then_inc(x_hi, 1)
                if k == 3:
                    split_hi(0, 0, 0, 1)
            act.wait_ge(consts_in[0], 16)
            act.wait_ge(made, 6)
            with act.Fori(0, 2) as it:
                for jj in range(4):
                    for i in range(3):
                        m = 3 * jj + i
                        split_hi(0, it, 12, m + 2)
                        if i == 0:
                            act.wait_ge(proj_done, it * 12 + m + 1)
                            act.activation(sg[:, jj % 2, :], tok(m % 2), ACT.Sigmoid).then_inc(gate_done, 1)
                        if i == 2:
                            act.wait_ge(proj_done, it * 12 + m + 1)
                            act.activation(zs[:, bass.ds(it * 4 + jj, 1), :].rearrange("p a n -> p (a n)"),
                                           tok(m % 2), ACT.Copy).then_inc(z_done, 1)
                    j = it * 4 + jj
                    act.wait_ge(u_done, 2 * j + 4)
                    for w in range(ACT_TAPS):
                        x = u_in[:, bass.ds(j, 1), w:w + SEQ].rearrange("p a n -> p (a n)")
                        of_chunk = lambda c: vec[:, bass.ds(j, 1), c:c + 1].rearrange("p a n -> p (a n)")
                        if w == 0:
                            act.wait_ge(conv_merged, 2 * j + 2)
                            act.activation(pool_sum[:, jj % 2, :], x, ACT.Identity, scale=of_chunk(w),
                                           bias=of_chunk(V_DWB)).then_inc(tap_done, 1)
                        else:
                            act.wait_ge(tap_added, j * (ACT_TAPS - 1) + w)
                            act.activation(tap_prod[:, w - 1, :], x, ACT.Copy, scale=of_chunk(w)).then_inc(tap_done, 1)
            act.wait_ge(z_done, 1 + KC)
            for k in range(KC):
                act.activation(zs[:, k, :], zs[:, k, :], ACT.Silu).then_inc(silu_done, 1)
            norm(0)
            act.wait_ge(u_stored, 16 * 2 * KC)
            for k in range(KC + 1):
                if k < KC:
                    act.wait_ge(ln_scaled, k + 1)
                    if k >= 2:
                        act.wait_ge(gated, 2 * (k - 1))
                    act.activation(sg[:, k % 2, :], res[:, k, :], ACT.Silu, bias=vec[:, k, V_LNB:V_LNB + 1],
                                   scale=vec[:, k, V_LNG:V_LNG + 1]).then_inc(ln_act, 1)
                if k:
                    act.wait_ge(gated, 2 * k)
                    act.activation(mid_hi[:, k - 1, :], res[:, k - 1, :], ACT.Copy).then_inc(mid_hi_done, 1)
            with act.Fori(0, 2) as it:
                for m in range(4):
                    split_hi(N_OUT0, it, 4, m + 2)
            norm(1)
            for k in range(KC):
                act.wait_ge(ln_scaled, KC + k + 1)
                act.activation(res[:, k, :], res[:, k, :], ACT.Identity, bias=vec[:, k, V_B0:V_B0 + 1],
                               scale=vec[:, k, V_G0:V_G0 + 1]).then_inc(ln_act, 1)
                act.wait_ge(ln_act, KC + k + 1)
                act.activation(act_hi[:, k, :], res[:, k, :], ACT.Copy).then_inc(x_hi, 1)

            def exp_rows(hg, bh):
                act.wait_ge(ss_max, hg * 2 + bh + 1)
                act.activation(s_probs[:, bh, :], s_probs[:, bh, :], ACT.Exp, scale=-1.0,
                               bias=s_neg_top[:, bh:bh + 1], accum_out=s_total[:, bh:bh + 1]).then_inc(ss_exp, 1)

            def group(hg, first):
                for ch in range(2):
                    chunk = hg * 2 + ch

                    def exp(u):
                        act.wait_ge(s_max, chunk * 8 + u + 1)
                        act.activation(probs[:, u % 2, :], probs[:, u % 2, :], ACT.Exp, scale=-1.0,
                                       bias=neg_top[:, u % 2:u % 2 + 1],
                                       accum_out=total[:, u % 2:u % 2 + 1]).then_inc(s_exp, 1)

                    def probs_out(u):
                        act.wait_ge(pt_done, chunk * 8 + u + 1)
                        if u >= 2:
                            act.wait_ge(o_done, chunk * 4 + u // 2)
                        act.activation(probsT[:, u % 2, :], C[:, 0:PW], ACT.Copy).then_inc(pt_out, 1)

                    for i in range(U_CH):
                        m = ch * U_CH + i
                        kind, g = KINDS[i]
                        if m == 6 and not first:
                            exp_rows(hg - 1, 0)
                        if i < U_CH - 2:
                            split_hi(N_IN1, hg, U_HG, m + 2)
                        if i == U_CH - 1:
                            exp(0)
                            exp(1)
                            if ch == 0 and not first:
                                exp_rows(hg - 1, 1)
                        act.wait_ge(proj_done, N_IN1 + hg * U_HG + m + 1)
                        kept = dict(z=z_new[:, ch, :], q=q_new[:, g, ch, :], k=k_new[:, g, ch, :], v=None)[kind]
                        if m == 0 and not first:
                            act.wait_ge(handed, hg)
                        if kept is not None:
                            act.activation(kept, tok(m % 2, 0, NS), ACT.Silu if kind == "z" else ACT.Copy)
                        if kind == "z":
                            if not (first and ch == 0):
                                act.wait_ge(o_out, chunk * 4)
                            act.activation(zT[:, :], tok(m % 2), ACT.Silu).then_inc(qkv_out, 1)
                        elif kind == "q":
                            act.activation(qT[:, g, :], tok(m % 2), ACT.Copy).then_inc(qkv_out, 1)
                        elif kind == "k":
                            act.wait_ge(k_stored[g], 16 + 16 * chunk)
                            act.activation(kT[:, g, :], tok(m % 2), ACT.Copy).then_inc(qkv_out, 1)
                        else:
                            act.wait_ge(v_stored[g % 2], 16 + 16 * (chunk if g == 1 else chunk * 2 + g // 2))
                            act.activation(vT[:, g % 2, :], tok(m % 2), ACT.Copy).then_inc(qkv_out, 1)
                        if i >= U_CH - 2:
                            split_hi(N_IN1, hg, U_HG, m + 2)

                    for r in range(NCL):
                        probs_out(2 * r)
                        probs_out(2 * r + 1)
                        if r < NCL - 1:
                            exp(2 * r + 2)
                            exp(2 * r + 3)

            group(0, True)
            with act.Fori(1, HG) as hg:
                group(hg, False)
            act.wait_ge(o_out, HG * 8)
            for g in range(NG):
                act.wait_ge(k_stored[g], 16 + 16 * KC)
            act.wait_ge(v_stored[0], 16 + 16 * 2 * KC)
            act.wait_ge(v_stored[1], 16 + 16 * KC)
            for k in range(KC):
                act.activation(mid1_hi[:, k, :], res[:, k, NS:NT], ACT.Copy).then_inc(mid1_hi_done, 1)
            split_hi(N_OUT1, 0, 0, 2)
            exp_rows(HG - 1, 0)
            split_hi(N_OUT1, 0, 0, 3)
            split_hi(N_OUT1, 0, 0, 4)
            exp_rows(HG - 1, 1)
            for m in range(5, KC):
                split_hi(N_OUT1, 0, 0, m)
            act.wait_ge(ln_sum, 3)
            act.activation(neg_mean1[:, :], A[:, 512:512 + SEQ], ACT.Copy, scale=-1.0 / D).then_inc(ln_mean, 1)
            for k in range(KC):
                act.wait_ge(ln_cent, 2 * KC + k + 1)
                if k >= 2:
                    act.wait_ge(ln_sqsum, 2 * KC + k - 1)
                act.activation(sq1[:, k % 2, :], res[:, k, NS:NT], ACT.Square).then_inc(ln_sq, 1)
            act.wait_ge(ln_sqsum, 3 * KC)
            act.activation(std1[:, :], B[:, 512:512 + SEQ], ACT.Sqrt, scale=1.0 / D, bias=vec[:, 0, V_EPS:V_EPS + 1])\
                .then_inc(ln_std, 1)

            def scale_shift(x, k):
                return act.activation(x, x, ACT.Identity, bias=vec[:, k, V_B1:V_B1 + 1], scale=vec[:, k, V_G1:V_G1 + 1])

            for k in range(KC):
                act.wait_ge(ln_scaled, 2 * KC + k + 1)
                scale_shift(res[:, k, NS:NT], k).then_inc(ln_act, 1)
            act.wait_ge(ln_sum, 4)
            act.activation(neg_mean1[:, 0:NS], C[:, 0:NS], ACT.Copy, scale=-1.0 / D).then_inc(sample_out, 1)
            act.wait_ge(sample_out, 4)
            act.activation(ys_sq[:, :, :], ys[:, :, :], ACT.Square).then_inc(sample_out, 1)
            act.wait_ge(ln_sqsum, 3 * KC + 1)
            act.activation(std1[:, 0:NS], C[:, 512:512 + NS], ACT.Sqrt, scale=1.0 / D, bias=vec[:, 0, V_EPS:V_EPS + 1])\
                .then_inc(sample_out, 1)
            act.wait_ge(sample_out, 8)
            for k in range(KC):
                scale_shift(ys[:, k, :], k).then_inc(sample_out, 1)

        @block.gpsimd
        def _(pool):
            def lo(dst, src, hi):
                return pool.tensor_tensor(dst, src, hi.bitcast(F32), ALU.subtract)

            def split_lo(base, it, per, m):
                pool.wait_ge(hi_done, base + it * per + m + 1)
                lo(w_lo[:, m % 2, :], landing[:, m % LAND, :], w_hi[:, m % 2, :]).then_inc(w_split, 1)

            pool.sem_inc(w_split, LAND)
            pool.sem_inc(z_done, 1)
            pool.sem_inc(u_done, 2)
            pool.sem_inc(res_part, 2)
            pool.sem_inc(tile_used, RING)
            pool.sem_inc(tap_added, ACT_TAPS - 1)
            pool.sem_inc(conv_merged, 4)
            for s in (*k_stored, *v_stored):
                pool.sem_inc(s, 16)
            pool.memset(ones[:, :], 1.0).then_inc(made, 1)
            pool.memset(u_in[:, :, 0:HALO], 0.0).then_inc(made, 5)
            pool.wait_ge(made, 6)

            split_lo(0, 0, 0, 0)
            split_lo(0, 0, 0, 1)

            def add_taps(j, ws):
                for w in ws:
                    n = j * (ACT_TAPS - 1) + w
                    pool.wait_ge(tap_done, j * ACT_TAPS + w + 1)
                    pool.wait_ge(tap_added, n - 1 + ACT_TAPS - 1)
                    acc = pool_sum[:, j % 2, :]
                    pool.tensor_tensor(acc, acc, tap_prod[:, w - 1, :], ALU.add).then_inc(tap_added, 1)

            def sample_products(j):
                if j == 0:
                    pool.wait_ge(state_in, 16)
                    pool.wait_ge(consts_in[0], 16)
                else:
                    pool.wait_ge(sconv, 2 * j - 1)
                first = u_in[:, j, US:US + NS]
                windows = bass.AP(tensor=first.tensor, offset=first.offset, ap=[first.ap[0], [NB, W], [1, NS]])
                taps = vec[:, j, 0:W].unsqueeze(2).to_broadcast([P, W, NS])
                pool.tensor_tensor(prod[:, :, :], windows, taps, ALU.mult).then_inc(prod_done, 1)

            for j in range(KC):
                for i in range(3):
                    split_lo(0, 0, 0, 3 * j + i + 2)
                    if j:
                        add_taps(j - 1, range((1, 3, 5)[i], (3, 5, ACT_TAPS)[i]))
                if j:
                    sample_products(j - 1)
            add_taps(KC - 1, range(1, ACT_TAPS))
            sample_products(KC - 1)
            for k in range(KC):
                pool.wait_ge(mid_hi_done, k + 1)
                lo(mid_lo[:, k, :], res[:, k, :], mid_hi[:, k, :]).then_inc(mid_split, 1)
            with pool.Fori(0, 2) as it:
                for m in range(4):
                    split_lo(N_OUT0, it, 4, m + 2)
            for k in range(0, KC, 2):
                pool.wait_ge(x_hi, KC + k + 1)
                lo(act_lo[:, k, :], res[:, k, :], act_hi[:, k, :]).then_inc(y_split[0], 1)
            pool.wait_ge(x_hi, 2 * KC)
            pool.memset(q_row[:, :, :, :, :, :], 0.0).then_inc(rows_cleared, 1)
            pool.memset(p_col[:, :, :], 0.0).then_inc(rows_cleared, 1)
            with pool.Fori(0, HG) as hg:
                for ch in range(2):
                    for i in range(U_CH):
                        split_lo(N_IN1, hg, U_HG, ch * U_CH + i + 2)
            for k in range(0, KC, 2):
                pool.wait_ge(mid1_hi_done, k + 1)
                lo(mid1_lo[:, k, :], res[:, k, NS:NT], mid1_hi[:, k, :]).then_inc(mid1_split[0], 1)
            for m in range(2, KC):
                split_lo(N_OUT1, 0, 0, m)

        @block.vector
        def _(dve):
            def by_class(x):
                return x.rearrange("p (i c) -> p c i", c=NCL)

            def of_class(x):
                return x.rearrange("p (c i) -> p c i", c=NCL)

            def value(j):
                s = (3 * j + 1) % 2
                dve.wait_ge(proj_done, 3 * j + 2)
                dve.wait_ge(gate_done, j + 1)
                dve.tensor_tensor(u_in[:, j, US + HALO * NB:UW], tok(s, 0, NS), sg[:, j % 2, 0:NS], ALU.mult)\
                    .then_inc(u_done, 1)
                dve.tensor_tensor(by_class(u_in[:, j, HALO:US]), of_class(tok(s, NS, NT)), of_class(sg[:, j % 2, NS:NT]),
                                  ALU.mult).then_inc(u_done, 1)

            def taps(j, lo_, hi_):
                if lo_ == 0:
                    dve.wait_ge(u_done, 2 * j + 4)
                for i in range(lo_, hi_):
                    w, q = ACT_TAPS + i, j * DVE_TAPS + i
                    x, acc = u_in[:, j, w:w + SEQ], odd_sum[:, j % 2, :] if i % 2 else res[:, j, NS:NT]
                    if i < 2:
                        dve.tensor_scalar(acc, x, vec[:, j, w:w + 1], None, ALU.mult).then_inc(conv, 1)
                    else:
                        dve.wait_ge(conv, q - 1)
                        dve.scalar_tensor_tensor(out=acc, in0=x, scalar=vec[:, j, w:w + 1], in1=acc,
                                                 op0=ALU.mult, op1=ALU.add).then_inc(conv, 1)

            def merge(j):
                acc = res[:, j, NS:NT]
                dve.wait_ge(conv, (j + 1) * DVE_TAPS)
                dve.tensor_tensor(acc, acc, odd_sum[:, j % 2, :], ALU.add).then_inc(conv_merged, 1)
                dve.wait_ge(conv_merged, 4 + 2 * j + 1)
                dve.wait_ge(tap_added, (j + 2) * (ACT_TAPS - 1))
                dve.tensor_tensor(acc, acc, pool_sum[:, j % 2, :], ALU.add).then_inc(conv_merged, 1)

            def sample_taps(j):
                dve.wait_ge(prod_done, j + 1)
                dve.tensor_reduce(res[:, j, 0:NS], prod[:, :, :].rearrange("p w n -> p n w"), mybir.AxisListType.X,
                                  ALU.add).then_inc(sconv, 1)
                dve.wait_ge(sconv, 2 * j + 1)
                dve.tensor_scalar(res[:, j, 0:NS], res[:, j, 0:NS], vec[:, j, V_DWB:V_DWB + 1], None, ALU.add)\
                    .then_inc(sconv, 1)

            def norm_begin(round_):
                dve.wait_ge(ln_mean, round_ + 1)
                for k in range(KC):
                    dve.tensor_tensor(res[:, k, :], res[:, k, :], neg_mean[:, :], ALU.add).then_inc(ln_cent, 1)
                dve.wait_ge(ln_std, round_ + 1)
                dve.reciprocal(rstd[:, :], std[:, :]).then_inc(ln_rstd, 1)
                dve.wait_ge(ln_rstd, round_ + 1)

            def norm_scale(k):
                dve.tensor_tensor(res[:, k, :], res[:, k, :], rstd[:, :], ALU.mult).then_inc(ln_scaled, 1)

            def lo(dst, src, hi):
                return dve.tensor_tensor(dst, src, hi.bitcast(F32), ALU.subtract)

            def residual(it, m, base, round_):
                at = bass.ds(it * 4 + m, 1)
                flat = lambda x: x[:, at, :].rearrange("p a n -> p (a n)")
                n = KC * round_ + it * 4 + m
                dve.wait_ge(proj_done, base + it * 4 + m + 1)
                dve.scalar_tensor_tensor(out=flat(res), in0=flat(act_hi).bitcast(F32), scalar=ALPHA, in1=tok(m % 2),
                                         op0=ALU.mult, op1=ALU.add).then_inc(res_part, 1)
                dve.wait_ge(res_part, n + 3)
                dve.scalar_tensor_tensor(out=flat(res), in0=flat(act_lo).bitcast(F32), scalar=ALPHA, in1=flat(res),
                                         op0=ALU.mult, op1=ALU.add).then_inc(res_done, 1)

            for k in range(KC):
                dve.wait_ge(x_hi, k + 1)
                lo(act_lo[:, k, :], res[:, k, :], act_hi[:, k, :]).then_inc(x_split, 1)
            dve.wait_ge(made, 6)
            dve.wait_ge(consts_in[0], 16)
            dve.wait_ge(x_split, KC)
            value(0)
            for j in range(KC):
                taps(j, 0, DVE_TAPS)
                if j < KC - 1:
                    value(j + 1)
                if j:
                    merge(j - 1)
                    sample_taps(j - 1)
            merge(KC - 1)
            sample_taps(KC - 1)
            norm_begin(0)

            def gate(k):
                dve.wait_ge(ln_act, k + 1)
                dve.wait_ge(silu_done, k + 1)
                dve.tensor_tensor(res[:, k, 0:NS], sg[:, k % 2, 0:NS], zs[:, k, 0:NS], ALU.mult).then_inc(gated, 1)
                dve.tensor_tensor(of_class(res[:, k, NS:NT]), by_class(sg[:, k % 2, NS:NT]), of_class(zs[:, k, NS:NT]),
                                  ALU.mult).then_inc(gated, 1)

            norm_scale(0)
            norm_scale(1)
            for k in range(KC):
                gate(k)
                if k + 2 < KC:
                    norm_scale(k + 2)
            with dve.Fori(0, 2) as it:
                for m in range(4):
                    residual(it, m, N_OUT0, 0)
            norm_begin(1)
            for k in range(KC + 3):
                if k < KC:
                    norm_scale(k)
                if k >= 4 and k % 2 == 0:
                    dve.wait_ge(x_hi, KC + k - 2)
                    lo(act_lo[:, k - 3, :], res[:, k - 3, :], act_hi[:, k - 3, :]).then_inc(y_split[1], 1)

            for i in range(1, 6):
                dve.wait_ge(consts_in[i], 16)
            dve.wait_ge(rows_cleared, 2)
            def q_fill(hg, bh, g):
                if bh:
                    dve.wait_ge(tile_used, RING + hg * TILES_HG + (1, 5, TILES)[g])
                for ch in range(2):
                    for half in range(2):
                        rows, h = slice(HD * half, HD * half + HD), 2 * ch + half
                        src = q_old[rows, g, ch, :].rearrange("p (q b) -> p b q", b=NB)[:, 4 * bh:4 * bh + 4, :]
                        to = lambda t: q_row[rows, t, ch, :, h, :]
                        last = dve.tensor_copy(to((0, TILES, TILES + 1)[g]), src)
                        tiles = (0, 4, 8)[g]
                        for r in range(tiles):
                            last = dve.tensor_copy(to(FIRST_OF[g] + r)[:, :, r::tiles], src[:, :, r::tiles])
                last.then_inc(q_rows, 1)

            def largest_rows(hg, bh):
                S = pair[2 + bh]
                dve.wait_ge(tile_used, RING + hg * TILES_HG + (bh + 1) * TILES)
                dve.memset(s_part[:, bh:bh + 1], 0.0)
                dve.tensor_tensor_reduce(s_probs[:, bh, :], S[:, P:P + SW], mask_s[:, bh, :], -SCALE, -NEG,
                                         ALU.add, ALU.min, s_neg_top[:, bh:bh + 1]).then_inc(ss_max, 1)

            def normalise_rows(hg, bh):
                n = hg * 2 + bh + 1
                dve.wait_ge(ss_exp, n)
                dve.reciprocal(s_part[:, bh:bh + 1], s_total[:, bh:bh + 1]).then_inc(ss_share, 1)
                dve.wait_ge(ss_share, n)
                dve.tensor_scalar(s_probs[:, bh, :], s_probs[:, bh, :], s_part[:, bh:bh + 1], None, ALU.mult)\
                    .then_inc(ss_norm, 1)

            def p_fill(hg, bh, T, g):
                if g == 0:
                    dve.wait_ge(spt_done, hg * 2 + bh + 1)
                if bh:
                    dve.wait_ge(tile_used, RING + hg * TILES_HG + 2 * TILES + (1, 5, TILES)[g])
                rows = lambda x: x.rearrange("p (m q) -> p m q", q=NQ)
                if g == 0:
                    dve.tensor_copy(p_new[:, :, :].rearrange("p g m -> p (g m)"), T[0:NS, 512:512 + NG * P])\
                        .then_inc(p_cols, 1)
                    last = dve.tensor_copy(p_col[:, 0, :], T[:, 0:P])
                tiles = (0, 4, 8)[g]
                for r in range(tiles):
                    last = dve.tensor_copy(rows(p_col[:, FIRST_OF[g] + r, :])[:, :, r::tiles],
                                           rows(T[:, g * P:(g + 1) * P])[:, :, r::tiles])
                last.then_inc(p_cols, 1)

            def own_heads(hg, bh):
                dve.wait_ge(tile_used, RING + hg * TILES_HG + (bh + 3) * TILES)
                if bh:
                    dve.wait_ge(sot_done, hg * 2 + 1)
                dve.tensor_tensor(o_own[:, :], C[:, 0:2 * P], head_mask[:, :], ALU.mult).then_inc(so_own, 1)

            def gate_rows(hg, bh):
                dve.wait_ge(sot_done, hg * 2 + bh + 1)
                for ch in range(2):
                    cols = lambda x: x.rearrange("p (q b) -> p b q", b=NB)[:, 4 * bh:4 * bh + 4, :]
                    dve.tensor_tensor(cols(res[:, bass.ds(hg * 2 + ch, 1), 0:NS].rearrange("p a n -> p (a n)")),
                                      C[:, 512 + ch * 4 * NQ:512 + (ch + 1) * 4 * NQ].rearrange("p (b q) -> p b q", b=4),
                                      cols(z_old[:, ch, :]), ALU.mult).then_inc(sot_out, 1)

            def hand_over(hg):
                dve.wait_ge(qkv_out, (hg + 1) * U_HG)
                dve.wait_ge(v_ready, (hg + 1) * 12)
                dve.tensor_copy(q_old[:, :, :, :], q_new[:, :, :, :]).then_inc(handing, 1)
                dve.tensor_copy(k_old[:, :, :, :], k_new[:, :, :, :]).then_inc(handing, 1)
                dve.tensor_copy(v_old[:, :, :], v_new[:, :, :]).then_inc(handing, 1)
                dve.tensor_copy(z_old[:, :, :], z_new[:, :, :]).then_inc(handed, 1)

            def group(hg, first):
                def v_out(ch, g):
                    V = DD if g == 2 else A
                    dve.wait_ge(vt_done, (hg * 2 + ch) * NG + g + 1)
                    dve.tensor_copy(v_nat[:, g, :, :].rearrange("p c n -> p (c n)"), V[:, 0:512]).then_inc(v_ready, 1)
                    dve.tensor_copy(v_new[:, g, ch * P:(ch + 1) * P], V[0:NS, 512:512 + P]).then_inc(v_ready, 1)

                def largest(ch, u):
                    su, s = (hg * 2 + ch) * 8 + u, u % 2
                    dve.wait_ge(s_done, su + 1)
                    if u >= 2:
                        dve.wait_ge(pt_done, su - 1)
                    dve.memset(share[:, s:s + 1], 0.0)
                    dve.tensor_tensor_reduce(probs[:, s, :], score_pair(ch, u)[:, 0:PW], mask_p[:, u // 2, :], -SCALE, -NEG,
                                             ALU.add, ALU.min, neg_top[:, s:s + 1]).then_inc(s_max, 1)

                def normalise(ch, u):
                    su, s = (hg * 2 + ch) * 8 + u, u % 2
                    dve.wait_ge(s_exp, su + 1)
                    dve.reciprocal(share[:, s:s + 1], total[:, s:s + 1]).then_inc(s_share, 1)
                    dve.wait_ge(s_share, su + 1)
                    dve.tensor_scalar(probs[:, s, :], probs[:, s, :], share[:, s:s + 1], None, ALU.mult)\
                        .then_inc(s_norm, 1)

                def gate_out(ch, r):
                    dve.wait_ge(o_done, (hg * 2 + ch) * 4 + r + 1)
                    own = NS + r * P
                    dve.tensor_tensor(res[:, bass.ds(hg * 2 + ch, 1), own:own + P].rearrange("p a n -> p (a n)"),
                                      DD[:, 0:P], zT[:, own:own + P], ALU.mult).then_inc(o_out, 1)

                for ch in range(2):
                    chunk = hg * 2 + ch
                    if first:
                        v_out(ch, 0)
                        v_out(ch, 1)
                        largest(ch, 0)
                        largest(ch, 1)
                    elif ch == 0:
                        v_out(ch, 0)
                        largest_rows(hg - 1, 0)
                        for g in range(NG):
                            q_fill(hg - 1, 1, g)
                        v_out(ch, 1)
                        normalise_rows(hg - 1, 0)
                        largest(ch, 0)
                        largest(ch, 1)
                        largest_rows(hg - 1, 1)
                    else:
                        normalise_rows(hg - 1, 1)
                        for g in range(NG):
                            p_fill(hg - 1, 0, DD, g)
                        v_out(ch, 0)
                        own_heads(hg - 1, 0)
                        for g in range(NG):
                            p_fill(hg - 1, 1, DD, g)
                        gate_rows(hg - 1, 0)
                        v_out(ch, 1)
                        largest(ch, 0)
                        largest(ch, 1)
                        own_heads(hg - 1, 1)
                    normalise(ch, 0)
                    normalise(ch, 1)
                    if ch and not first:
                        gate_rows(hg - 1, 1)
                    for r in range(NCL):
                        if r < NCL - 1:
                            largest(ch, 2 * r + 2)
                            if r == 0:
                                v_out(ch, 2)
                            largest(ch, 2 * r + 3)
                            normalise(ch, 2 * r + 2)
                            normalise(ch, 2 * r + 3)
                            gate_out(ch, r)
                        if ch and r == 0:
                            hand_over(hg)
                        elif ch:
                            dve.wait_ge(handing, 3 * (hg + 1))
                            q_fill(hg, 0, r - 1)
                    gate_out(ch, NCL - 1)

            group(0, True)
            with dve.Fori(1, HG) as hg:
                group(hg, False)
            hg = HG - 1

            def prompt_residual(m):
                dve.wait_ge(proj_done, N_OUT1 + m + 1)
                dve.scalar_tensor_tensor(out=res[:, m, NS:NT], in0=act_hi[:, m, NS:NT].bitcast(F32), scalar=ALPHA,
                                         in1=pair[m % 2][:, 0:SEQ], op0=ALU.mult, op1=ALU.add).then_inc(res_part, 1)
                dve.wait_ge(res_part, KC + m + 3)
                dve.scalar_tensor_tensor(out=res[:, m, NS:NT], in0=act_lo[:, m, NS:NT].bitcast(F32), scalar=ALPHA,
                                         in1=res[:, m, NS:NT], op0=ALU.mult, op1=ALU.add).then_inc(res_done, 1)

            for k in range(1, KC, 2):
                dve.wait_ge(mid1_hi_done, k + 1)
                lo(mid1_lo[:, k, :], res[:, k, NS:NT], mid1_hi[:, k, :]).then_inc(mid1_split[1], 1)
            dve.wait_ge(mid1_split[0], KC // 2)
            q_fill(hg, 1, 0)
            q_fill(hg, 1, 1)
            prompt_residual(0)
            largest_rows(hg, 0)
            q_fill(hg, 1, 2)
            normalise_rows(hg, 0)
            prompt_residual(1)
            prompt_residual(2)
            largest_rows(hg, 1)
            prompt_residual(3)
            for g in range(NG):
                p_fill(hg, 0, DD, g)
            normalise_rows(hg, 1)
            prompt_residual(4)
            prompt_residual(5)
            own_heads(hg, 0)
            for g in range(NG):
                p_fill(hg, 1, DD, g)
            prompt_residual(6)
            gate_rows(hg, 0)
            prompt_residual(7)
            dve.wait_ge(ln_mean, 3)
            for k in range(KC):
                dve.tensor_tensor(res[:, k, NS:NT], res[:, k, NS:NT], neg_mean1[:, :], ALU.add).then_inc(ln_cent, 1)
            own_heads(hg, 1)
            gate_rows(hg, 1)
            dve.wait_ge(ln_std, 3)
            dve.reciprocal(rstd1[:, :], std1[:, :]).then_inc(ln_rstd, 1)
            dve.wait_ge(ln_rstd, 3)
            for k in range(KC):
                dve.tensor_tensor(res[:, k, NS:NT], res[:, k, NS:NT], rstd1[:, :], ALU.mult).then_inc(ln_scaled, 1)
            over = lambda x: x[:, 0:NS].unsqueeze(1).to_broadcast([P, KC, NS])
            dve.wait_ge(proj_done, UNITS + 1)
            dve.scalar_tensor_tensor(out=ys[:, :, :], in0=act_hi[:, :, 0:NS].bitcast(F32), scalar=ALPHA,
                                     in1=DD[:, 0:KC * NS].rearrange("p (k n) -> p k n", k=KC),
                                     op0=ALU.mult, op1=ALU.add).then_inc(sample_out, 1)
            dve.wait_ge(sample_out, 1)
            dve.scalar_tensor_tensor(out=ys[:, :, :], in0=act_lo[:, :, 0:NS].bitcast(F32), scalar=ALPHA,
                                     in1=ys[:, :, :], op0=ALU.mult, op1=ALU.add).then_inc(sample_out, 1)
            dve.wait_ge(sample_out, 3)
            dve.tensor_tensor(ys[:, :, :], ys[:, :, :], over(neg_mean1), ALU.add).then_inc(sample_out, 1)
            dve.wait_ge(sample_out, 6)
            dve.reciprocal(rstd1[:, 0:NS], std1[:, 0:NS]).then_inc(sample_out, 1)
            dve.wait_ge(sample_out, 7)
            dve.tensor_tensor(ys[:, :, :], ys[:, :, :], over(rstd1), ALU.mult).then_inc(sample_out, 1)


def constants():
    i = np.arange(P)
    mask_p = np.full((P, NCL, PW), NEG, np.float32)
    for r in range(NCL):
        for c in range(NCL):
            back = 4 * (i[:, None] - i[None, :]) + r - c
            mask_p[:, r, c * P:(c + 1) * P][(back >= 0) & (back <= WIN[0])] = 0
        back = i[:, None] - i[None, :]
        mask_p[:, r, 4 * P:5 * P][back >= 0] = 0
        mask_p[:, r, 5 * P:6 * P][(back >= 0) & (back % 4 == 0)] = 0
    row = np.arange(P)
    b4, h, q = row // 32, row // 8 % 4, row % 8
    mask_s = np.zeros((P, 2, SW), np.float32)
    mask_s[:, :, 0:P][(i[None, :] < q[:, None])[:, None, :].repeat(2, 1)] = NEG
    mask_s[:, :, P:2 * P][(i[None, :] < q[:, None] // 4)[:, None, :].repeat(2, 1)] = NEG
    n = np.arange(NS)
    t, b = n // NB, n % NB
    for bh in range(2):
        same = b[None, :] == 4 * bh + b4[:, None]
        back = q[:, None] - t[None, :]
        for g in range(NG):
            ok = same & (back >= 0) & (back % DIL[g] == 0)
            mask_s[:, bh, NG * P + g * NS:NG * P + (g + 1) * NS][~ok] = NEG
    head_mask = (np.arange(2 * P)[None, :] // HD == h[:, None]).astype(np.float32)
    pick = np.zeros((P, 4 * NQ), np.float32)
    pick[row, b4 * NQ + q] = 1
    return dict(ident=np.eye(P, dtype=np.float32), mask_p=mask_p, mask_s=mask_s, head_mask=head_mask, pick=pick)


def units(*weights):
    return [np.ascontiguousarray(w.reshape(KC, P, P).transpose(1, 0, 2)).reshape(P, KC * P) for w in weights]


def kernel(**inputs):
    from concourse import bacc
    from concourse.bass_utils import run_bass_kernel_spmd

    x = {k: np.asarray(v) for k, v in inputs.items()}
    w0, w1 = x["conv_w_in"][0], x["attn_w_in"][0]
    cols = lambda w, at: w[:, at:at + P]
    order = [cols(w0, base + j * P) for j in range(KC) for base in (D, 0, 2 * D)]
    order += [cols(x["conv_w_out"][0], j * P) for j in range(KC)]
    place = lambda kind, g: NG * 3 if kind == "z" else 3 * g + "qkv".index(kind)
    order += [cols(w1, place(*kind) * D + j * P) for j in range(KC) for kind in KINDS]
    order += [cols(x["attn_w_out"][0], j * P) for j in range(KC)]
    arrays = dict(constants())
    arrays["w_units"] = np.stack(units(*order))

    prompt = x["x_prompt"][0].reshape(P, NCL, D).transpose(1, 0, 2).reshape(SEQ, D)
    sample = x["x_sample"].transpose(1, 0, 2).reshape(NS, D)
    chunks = lambda a: np.ascontiguousarray(a.reshape(a.shape[0], KC, P).transpose(2, 1, 0))
    arrays["xT"] = chunks(np.concatenate([sample, prompt]))
    arrays["vec"] = chunks(np.concatenate([x["conv_dw_w"][0], x["conv_dw_b"], x["conv_ln_g"], x["conv_ln_b"],
                                           x["norm_g"][0:1], x["norm_b"][0:1], x["norm_g"][1:2], x["norm_b"][1:2],
                                           np.full((1, D), EPS, np.float32)]))
    arrays["state"] = chunks(x["state_conv"][0].transpose(1, 0, 2).reshape(HALO * NB, D))
    k_tiles, v_tiles = [], []
    caches = [x[f"cache_kv_w{w}_d{dil}"][0] for w, dil in zip(WIN, DIL)]
    for g, c in enumerate(caches):
        arrays[f"cache{g}"] = c.reshape(NB, WIN[g] * 2 * D)
        c = c.reshape(2, 4, P, DIL[g], 2, HG, 2 * P)[:, :, :, 0:8]
        k_tiles.append(c[:, :, :, :, 0].reshape(2, 4, P, -1, HG, 2, P).transpose(4, 0, 3, 6, 5, 1, 2))
        v_tiles.append(c[:, :, :, :, 1].transpose(4, 0, 3, 2, 1, 5))
    arrays["k_tiles"] = np.concatenate([a.reshape(HG, 2, -1, P, 2 * 4 * P) for a in k_tiles], 2).reshape(-1, P, 2 * 4 * P)
    arrays["v_tiles"] = np.concatenate([a.reshape(HG, 2, -1, P, 2 * 4 * P) for a in v_tiles], 2).reshape(-1, P, 2 * 4 * P)

    nc = bacc.Bacc("TRN2", target_bir_lowering=False, num_devices=1)
    d = {n: nc.dram_tensor(n, a.shape, F32, kind="ExternalInput").ap() for n, a in arrays.items()}
    shapes = dict(yT=(P, KC, NT), kv_new=(KC * NG * 2, P, NT), conv_p=(P, KC, HALO), conv_s=(P, KC, HALO * NB),
                  **{f"kept{g}": (NB, (WIN[g] - NQ) * 2 * D) for g in range(NG)})
    o = {n: nc.dram_tensor(n, s, F32, kind="ExternalOutput").ap() for n, s in shapes.items()}
    build(nc, d, o)
    got = run_bass_kernel_spmd(nc, [arrays], core_ids=[0]).results[0]

    def tokens(a):
        a = np.moveaxis(a, -1, -2)
        s, p = a[..., :NS, :], a[..., NS:, :]
        p = np.swapaxes(p.reshape(*a.shape[:-2], NCL, P, D), -3, -2).reshape(*a.shape[:-2], SEQ, D)
        return p, np.swapaxes(s.reshape(*a.shape[:-2], NQ, NB, D), -3, -2)

    yp, ys = tokens(got["yT"].transpose(1, 0, 2).reshape(D, NT))
    kv = got["kv_new"].reshape(KC, NG, 2, P, NT).transpose(1, 2, 0, 3, 4).reshape(NG, 2, D, NT)
    kvp, kvs = tokens(kv)
    heads = lambda a: a.reshape(*a.shape[:-1], D // HD, HD)
    out_p, out_s = [], []
    for g in range(NG):
        keep = min(WIN[g], SEQ)
        out_p.append(heads(kvp[g].transpose(1, 0, 2))[None, None, -keep:])
        new = heads(kvs[g].transpose(1, 2, 0, 3))
        out_s.append(np.concatenate([got[f"kept{g}"].reshape(NB, WIN[g] - NQ, 2, D // HD, HD), new], 1)[None])
    conv_p = got["conv_p"].transpose(2, 1, 0).reshape(1, 1, HALO, D)
    conv_s = got["conv_s"].transpose(2, 1, 0).reshape(HALO, NB, D).transpose(1, 0, 2)[None]
    c = np.ascontiguousarray
    return (c(yp[None]), c(ys), *map(c, out_p), c(conv_p), *map(c, out_s), c(conv_s))
```

```python
from contextlib import ExitStack

import concourse.bass as bass
from concourse import mybir
import numpy as np

F32 = mybir.dt.float32
F32R = mybir.dt.float32r
ALU = mybir.AluOpType
ACT = mybir.ActivationFunctionType

P = 128
D = 1024
KC = D // P
SEQ = 512
NB = 8
NQ = 8
NS = NB * NQ
NT = NS + SEQ
NCL = 4
W = 31
HALO = W - 1
HD = 64
NG = 3
WIN = (128, 512, 2048)
DIL = (1, 4, 16)
HG = 4
TILES = 1 + 4 + 8
GROUP_OF = [0] + [1] * 4 + [2] * 8
FIRST_OF = (0, 1, 5)
SCALE = HD ** -0.5
ALPHA = 4.0 ** 0.25
EPS = 1e-5
NEG = -1e30

U_IN0 = 3 * KC
U_OUT0 = KC
KINDS = [("q", 0), ("k", 0), ("v", 0), ("z", 0), ("q", 1), ("k", 1), ("v", 1), ("q", 2), ("k", 2), ("v", 2)]
U_CH = len(KINDS)
U_HG = 2 * U_CH
N_OUT0 = U_IN0
N_IN1 = U_IN0 + U_OUT0
N_OUT1 = N_IN1 + HG * U_HG
UNITS = N_OUT1 + KC
LAND = 4
RING = 5
TILES_HG = 4 * TILES
STEPS = (3, 3, 3, 2, 2) + (4, 3, 3, 3, 0) + (0, 4, 3, 3, 3) + (4, 3, 3, 3, 0)
TAIL_AT = (0, 7, 13, 19, 26, 31, 35, 39, 43)
TAIL_LOADS = (8, 14, 20, 26)
SAMPLE_STEPS = 9 + KC
STEP_AT = [sum(STEPS[:m]) for m in range(U_HG + 1)]

T0 = 512 - NS - 2 * P
SPLIT = NS + 2 * P
V_DWB, V_LNG, V_LNB, V_G0, V_B0, V_G1, V_B1, V_EPS = range(W, W + 8)
NV = W + 8

SW = NG * P + NG * NS
PW = NCL * P + 2 * P
COPY_ROWS = (120, 252, 255)
COPY_RUNS = (16, 32, 32)
UW = HALO + SEQ + (HALO + NQ) * NB
US = HALO + SEQ

ACT_TAPS = 8
DVE_TAPS = W - ACT_TAPS


def build(nc, d, o):
    with ExitStack() as ctx:
        def sb(name, shape, dt=F32, where=ctx):
            return where.enter_context(nc.sbuf_tensor(name, shape, dt))

        def sem(name):
            return ctx.enter_context(nc.semaphore(name))

        act_hi = sb("act_hi", [P, KC, NT], F32R)
        act_lo = sb("act_lo", [P, KC, NT], F32R)
        res = sb("res", [P, KC, NT])
        landing = sb("landing", [P, LAND, KC * P])
        w_hi = sb("w_hi", [P, 2, KC * P], F32R)
        w_lo = sb("w_lo", [P, 2, KC * P], F32R)
        ident = sb("ident_sb", [P, P])
        ones = sb("ones", [P, P])
        vec = sb("vec_sb", [P, KC, NV])
        mask_p = sb("mask_p_sb", [P, NCL, PW])
        mask_s = sb("mask_s_sb", [P, 2, SW])
        head_mask = sb("head_mask_sb", [P, 2 * P])
        pick = sb("pick_sb", [P, 4 * NQ])

        with ExitStack() as lay0:
            with ExitStack() as early:
                u_in = sb("u_in", [P, KC, UW], where=early)
                prod = sb("prod", [P, W, NS], where=early)
            mid_hi = sb("mid_hi", [P, KC, NT], F32R, where=lay0)
            mid_lo = sb("mid_lo", [P, KC, NT], F32R, where=lay0)
            zs = sb("zs", [P, KC, NT], where=lay0)
            sg = sb("sg", [P, 2, NT], where=lay0)
            neg_mean = sb("neg_mean", [P, NT], where=lay0)
            std = sb("std", [P, NT], where=lay0)
            rstd = sb("rstd", [P, NT], where=lay0)
            sq = sb("sq", [P, 2, NT], where=lay0)
            shift = sb("shift", [P, NT], where=lay0)
            odd_sum = sb("odd_sum", [P, 2, SEQ], where=lay0)
            pool_sum = sb("pool_sum", [P, 2, SEQ], where=lay0)
            tap_prod = sb("tap_prod", [P, ACT_TAPS - 1, SEQ], where=lay0)
        with ExitStack() as tail:
            mid1_hi = sb("mid1_hi", [P, KC, SEQ], F32R, where=tail)
            mid1_lo = sb("mid1_lo", [P, KC, SEQ], F32R, where=tail)
            ys = sb("ys", [P, KC, NS], where=tail)
            ys_sq = sb("ys_sq", [P, KC, NS], where=tail)
            neg_mean1 = sb("neg_mean1", [P, SEQ], where=tail)
            std1 = sb("std1", [P, SEQ], where=tail)
            rstd1 = sb("rstd1", [P, SEQ], where=tail)
            sq1 = sb("sq1", [P, 2, SEQ], where=tail)
        with ExitStack() as lay1:
            qT = sb("qT", [P, NG, NT], where=lay1)
            kT = sb("kT", [P, NG, NT], where=lay1)
            vT = sb("vT", [P, 2, NT], where=lay1)
            v_nat = sb("v_nat", [P, NG, NCL, P], where=lay1)
            zT = sb("zT", [P, NT], where=lay1)
            probs = sb("probs", [P, 2, PW], where=lay1)
            probsT = sb("probsT", [P, 2, PW], where=lay1)
            q_new = sb("q_new", [P, NG, 2, NS], where=lay1)
            k_new = sb("k_new", [P, NG, 2, NS], where=lay1)
            v_new = sb("v_new", [NS, NG, 2 * P], where=lay1)
            z_new = sb("z_new", [P, 2, NS], where=lay1)
            q_old = sb("q_old", [P, NG, 2, NS], where=lay1)
            k_old = sb("k_old", [P, NG, 2, NS], where=lay1)
            v_old = sb("v_old", [NS, NG, 2 * P], where=lay1)
            z_old = sb("z_old", [P, 2, NS], where=lay1)
            ring = sb("ring", [P, RING, 2 * 4 * P], where=lay1)
            q_row = sb("q_row", [P, TILES + 2, 2, 4, 4, NQ], where=lay1)
            s_probs = sb("s_probs", [P, 2, SW], where=lay1)
            p_col = sb("p_col", [P, TILES, P], where=lay1)
            p_new = sb("p_new", [NS, NG, P], where=lay1)
            o_own = sb("o_own", [P, 2 * P], where=lay1)
            neg_top = sb("neg_top", [P, 2], where=lay1)
            total = sb("total", [P, 2], where=lay1)
            share = sb("share", [P, 2], where=lay1)
            s_neg_top = sb("s_neg_top", [P, 2], where=lay1)
            s_total = sb("s_total", [P, 2], where=lay1)
            s_part = sb("s_part", [P, 2], where=lay1)

        pair = [ctx.enter_context(nc.psum_tensor(f"pair{x}", [P, 1024], F32)) for x in "ABCD"]
        A, B, C, DD = pair

        consts_in = [sem(f"consts_in{i}") for i in range(6)]
        x_in = [sem(f"x_in{h}") for h in range(4)]
        state_in = sem("state_in")
        w_landed = [sem(f"w_landed{s}") for s in range(LAND)]
        w_split = sem("w_split")
        hi_done = sem("hi_done")
        proj_done = sem("proj_done")
        x_hi = sem("x_hi")
        x_split = sem("x_split")
        y_split = [sem("y_split_pool"), sem("y_split_dve")]
        made = sem("made")
        gate_done = sem("gate_done")
        z_done = sem("z_done")
        silu_done = sem("silu_done")
        u_done = sem("u_done")
        prod_done = sem("prod_done")
        conv = sem("conv")
        tap_done = sem("tap_done")
        tap_added = sem("tap_added")
        pe_added = sem("pe_added")
        conv_merged = sem("conv_merged")
        sconv = sem("sconv")
        ln_sum = sem("ln_sum")
        ln_mean = sem("ln_mean")
        ln_cent = sem("ln_cent")
        ln_sq = sem("ln_sq")
        ln_sqsum = sem("ln_sqsum")
        ln_std = sem("ln_std")
        ln_rstd = sem("ln_rstd")
        ln_scaled = sem("ln_scaled")
        shift_sum = sem("shift_sum")
        shift_ready = sem("shift_ready")
        var_ready = sem("var_ready")
        off_mean = [sem("off_mean_dve"), sem("off_mean_pool")]
        ln_act = sem("ln_act")
        gated = sem("gated")
        mid1_hi_done = sem("mid1_hi_done")
        mid1_split = [sem("mid1_split_pool"), sem("mid1_split_dve")]
        sample_out = sem("sample_out")
        mid_hi_done = sem("mid_hi_done")
        mid_split = sem("mid_split")
        res_part = sem("res_part")
        res_done = sem("res_done")
        qkv_out = sem("qkv_out")
        vt_done = sem("vt_done")
        v_ready = sem("v_ready")
        s_done = sem("s_done")
        s_max = sem("s_max")
        s_exp = sem("s_exp")
        s_share = sem("s_share")
        s_norm = sem("s_norm")
        pt_done = sem("pt_done")
        pt_out = [sem("pt_out_even"), sem("pt_out_odd")]
        o_done = sem("o_done")
        o_out = sem("o_out")
        rows_cleared = sem("rows_cleared")
        handed = sem("handed")
        handing = sem("handing")
        q_rows = sem("q_rows")
        tile_in = [sem(f"tile_in{s}") for s in range(RING)]
        tile_used = sem("tile_used")
        ss_max = sem("ss_max")
        ss_exp = sem("ss_exp")
        ss_share = sem("ss_share")
        ss_norm = sem("ss_norm")
        spt_done = sem("spt_done")
        p_cols = sem("p_cols")
        so_own = sem("so_own")
        sot_done = sem("sot_done")
        sot_out = sem("sot_out")
        k_stored = [sem(f"k_stored{g}") for g in range(NG)]
        v_stored = [sem(f"v_stored{s}") for s in range(2)]
        u_stored = sem("u_stored")
        y_stored = sem("y_stored")
        copied = sem("copied")

        block = ctx.enter_context(nc.Block())

        def score_pair(ch, u):
            return pair[2 + ch] if u == 0 else A if u == 2 or u % 2 else B

        def turned_pair(u):
            return B if u in (1, 2 * NCL - 1) else C

        def tok(x, lo=0, hi=NT):
            return pair[x][:, T0 + lo:T0 + hi]

        @block.sync
        def _(sp):
            def load_unit(n, slot):
                sp.wait_ge(w_split, n + 1)
                sp.dma_start(landing[:, slot, :], d["w_units"][bass.ds(n, 1)].rearrange("a p m -> (a p) m"))\
                    .then_inc(w_landed[slot], 16)

            def copy_rows(g, b, piece):
                n = COPY_ROWS[g] * 2 * D
                src = d[f"cache{g}"][bass.ds(b, 1), (piece * n + NQ * 2 * D):(piece * n + NQ * 2 * D + n)]
                dst = o[f"kept{g}"][bass.ds(b, 1), piece * n:piece * n + n]
                sp.dma_start(dst.rearrange("a (r m) -> (a r) m", r=COPY_RUNS[g]),
                             src.rearrange("a (r m) -> (a r) m", r=COPY_RUNS[g])).then_inc(copied, 16)

            def store_u(j):
                sp.wait_ge(u_done, 2 * j + 4)
                sp.wait_ge(state_in, 16)
                sp.dma_start(o["conv_p"][:, j, :], u_in[:, j, SEQ:SEQ + HALO]).then_inc(u_stored, 16)
                sp.dma_start(o["conv_s"][:, j, :], u_in[:, j, US + NQ * NB:UW]).then_inc(u_stored, 16)

            def load_x(h):
                sp.dma_start(res[:, 2 * h:2 * h + 2, :], d["xT"][:, 2 * h:2 * h + 2, :]).then_inc(x_in[h], 16)

            def load_first(n):
                sp.dma_start(landing[:, n, :], d["w_units"][n]).then_inc(w_landed[n], 16)

            def load_const(i, dst, name):
                sp.dma_start(dst, d[name]).then_inc(consts_in[i], 16)

            load_first(0)
            for h in range(4):
                load_x(h)
                if h == 1:
                    load_first(1)
            load_const(0, vec[:, :, :], "vec")
            load_first(2)
            load_first(3)
            sp.wait_ge(made, 6)
            sp.dma_start(u_in[:, :, US:US + HALO * NB], d["state"]).then_inc(state_in, 16)
            for i, (dst, name) in enumerate(((ident[:, :], "ident"), (mask_p[:, :, :], "mask_p"),
                                             (mask_s[:, :, :], "mask_s"), (head_mask[:, :], "head_mask"),
                                             (pick[:, :], "pick"))):
                load_const(i + 1, dst, name)

            for j in range(KC):
                for i in range(3):
                    load_unit(3 * j + i + LAND, (3 * j + i) % LAND)
                    if i < 2:
                        copy_rows(2, j, i)
                if j:
                    store_u(j - 1)
            store_u(KC - 1)
            for b in range(NB):
                copy_rows(1, b, 0)
            with sp.Fori(0, 2) as it:
                for m in range(4):
                    load_unit(N_OUT0 + it * 4 + m + LAND, m)
                    copy_rows(2, it * 4 + m, 3)

            for ch in range(2):
                for piece in (6, 7):
                    copy_rows(2, ch, piece)
                copy_rows(2, KC - 2 + ch, 2)

            def load_tile(hg, t):
                last = t - RING if t >= RING else t - TILES_HG + (TILES_HG - 1 - t) // RING * RING
                sp.wait_ge(tile_used, RING + hg * TILES_HG + last + 1)
                which, tt = divmod(t, TILES)
                if which == 4:
                    sp.dma_start(ring[:, t % RING, :], d["w_units"][N_OUT1 + tt]).then_inc(tile_in[t % RING], 16)
                    return
                src = d["k_tiles" if which < 2 else "v_tiles"]
                sp.dma_start(ring[:, t % RING, :],
                             src[bass.ds((hg * 2 + which % 2) * TILES + tt, 1)].rearrange("a p m -> (a p) m"))\
                    .then_inc(tile_in[t % RING], 16)

            def store_kv(hg, m):
                ch, i = divmod(m, U_CH)
                kind, g = KINDS[i]
                if kind not in "kv":
                    return
                sp.wait_ge(qkv_out, hg * U_HG + m + 1)
                sp.dma_start(o["kv_new"][bass.ds((hg * 2 + ch) * 6 + g * 2 + "kv".index(kind), 1)]
                             .rearrange("a p n -> (a p) n"), kT[:, g, :] if kind == "k" else vT[:, g % 2, :])\
                    .then_inc(k_stored[g] if kind == "k" else v_stored[g % 2], 16)

            def load_group(hg, first):
                for m in range(U_HG):
                    ch, i = divmod(m, U_CH)
                    load_unit(N_IN1 + hg * U_HG + m + LAND, m % LAND)
                    if i:
                        store_kv(hg, m - 1)
                    if not first:
                        for t in range(STEP_AT[m], STEP_AT[m + 1]):
                            load_tile(hg - 1, t)
                    if i == U_CH - 1:
                        copy_rows(0, hg * 2 + ch, 0)
                        copy_rows(1, hg * 2 + ch, 1)
                    if first and i >= 2:
                        copy_rows(2, i - 2, 4 + ch)
                    if not first and i == U_CH - 1:
                        copy_rows(2, (hg - 1) * 2 + ch, 2)
                    if not first and i >= U_CH - 2:
                        copy_rows(2, hg * 2 + ch, 6 + i - (U_CH - 2))
                    if i == U_CH - 1:
                        store_kv(hg, m)

            load_group(0, True)
            with sp.Fori(1, HG) as hg:
                load_group(hg, False)
            for t in range(TILES_HG + LAND):
                load_tile(HG - 1, t)
                if t in TAIL_LOADS:
                    n = N_OUT1 + LAND + TAIL_LOADS.index(t)
                    load_unit(n, n % LAND)
            for k in range(KC):
                sp.wait_ge(ln_act, 2 * KC + k + 1)
                sp.dma_start(o["yT"][:, k, NS:NT], res[:, k, NS:NT]).then_inc(y_stored, 16)
            sp.wait_ge(sample_out, SAMPLE_STEPS)
            sp.dma_start(o["yT"][:, :, 0:NS], ys[:, :, :]).then_inc(y_stored, 16)
            sp.wait_ge(copied, 16 * NB * (1 + 2 + 8))
            for g in range(NG):
                sp.wait_ge(k_stored[g], 16 + 16 * KC)
            sp.wait_ge(v_stored[0], 16 + 16 * 2 * KC)
            sp.wait_ge(v_stored[1], 16 + 16 * KC)
            sp.wait_ge(u_stored, 16 * 2 * KC)
            sp.wait_ge(y_stored, 16 * (KC + 1))

        @block.tensor
        def _(pe):
            def unit(n, s, src_hi, src_lo, parts=None):
                pe.wait_ge(w_split, LAND + n + 1)
                for k in range(KC):
                    if parts is not None:
                        parts(k)
                    for q, (w, x) in enumerate(((w_hi, src_hi), (w_hi, src_lo), (w_lo, src_hi))):
                        first, last = k == 0 and q == 0, k == KC - 1 and q == 2
                        lhs = w[:, s, k * P:(k + 1) * P]
                        pe.matmul(tok(s, 0, SPLIT), lhs, x[:, k, 0:SPLIT], start=first, stop=last)
                        mm = pe.matmul(tok(s, SPLIT, NT), lhs, x[:, k, SPLIT:NT], start=first, stop=last)
                mm.then_inc(proj_done, 1)

            def norm_sum(k, last):
                pe.matmul(tok(2, 0, SPLIT), ones[:, :], res[:, k, 0:SPLIT], start=k == 0, stop=last)
                return pe.matmul(tok(2, SPLIT, NT), ones[:, :], res[:, k, SPLIT:NT], start=k == 0, stop=last)

            def norm_square(round_, k):
                pe.wait_ge(ln_sq, KC * round_ + k + 1)
                pe.matmul(tok(3, 0, SPLIT), ones[:, :], sq[:, k % 2, 0:SPLIT], start=k == 0, stop=k == KC - 1)
                pe.matmul(tok(3, SPLIT, NT), ones[:, :], sq[:, k % 2, SPLIT:NT], start=k == 0,
                          stop=k == KC - 1).then_inc(ln_sqsum, 1)

            def shifted_sums(k):
                pe.wait_ge(ln_cent, KC + k + 1)
                mm = norm_sum(k, k == KC - 1)
                if k == KC - 1:
                    mm.then_inc(ln_sum, 1)
                norm_square(1, k)

            pe.wait_ge(made, 6)
            with pe.Fori(0, 2) as it:
                for jj in range(4):
                    for i in range(3):
                        if i == 0:
                            pe.wait_ge(u_done, (it * 4 + jj) * 2 + 2)
                        elif i == 1:
                            pe.wait_ge(z_done, it * 4 + jj + 1)
                        else:
                            pe.wait_ge(gate_done, it * 4 + jj + 1)
                        unit(it * 12 + 3 * jj + i, (3 * jj + i) % 2, act_hi, act_lo,
                             (lambda k: pe.wait_ge(x_split, k + 1)) if i == jj == 0 else None)
            for k in range(KC):
                if k == KC - 2:
                    pe.wait_ge(consts_in[1], 16)
                    pe.wait_ge(u_done, 2 + 2 * KC)
                    for w in range(ACT_TAPS):
                        pe.wait_ge(tap_done, (KC - 1) * ACT_TAPS + w + 1)
                        mm = pe.matmul(A[:, 0:SEQ], ident[:, :], tap_prod[:, w - 1, :] if w else pool_sum[:, (KC - 1) % 2, :],
                                       start=w == 0, stop=w == ACT_TAPS - 1)
                    mm.then_inc(pe_added, 1)
                pe.wait_ge(conv_merged, 4 + 2 * (k + 1))
                pe.wait_ge(sconv, 2 * (k + 1))
                mm = norm_sum(k, k == KC - 1)
            mm.then_inc(ln_sum, 1)
            for k in range(KC):
                norm_square(0, k)
            pe.wait_ge(z_done, 1 + KC)
            for m in range(KC):
                pe.wait_ge(res_part, m + 1)
                unit(N_OUT0 + m, m % 2, mid_hi, mid_lo, (lambda k: pe.wait_ge(mid_split, k + 1)) if m == 0 else None)
                if m == 1:
                    pe.wait_ge(res_done, 1)
                    norm_sum(0, True).then_inc(shift_sum, 1)
                elif m > 1:
                    shifted_sums(m - 2)
            shifted_sums(KC - 2)
            shifted_sums(KC - 1)
            for i in range(1, 6):
                pe.wait_ge(consts_in[i], 16)

            def tile_ready(hg, t):
                slot, uses = t % RING, (TILES_HG - t % RING + RING - 1) // RING
                pe.wait_ge(tile_in[slot], (hg * uses + t // RING + 1) * 16)

            def score_rows(t, S, cols, first, last, keys):
                for ch in range(2):
                    for b in range(4):
                        mm = pe.matmul(S[32 * b:32 * b + 32, cols],
                                       q_row[:, t, ch, b, :, :].rearrange("p h q -> p (h q)"),
                                       keys(ch, b), start=first and ch == 0, stop=last and ch == 1)
                return mm

            def key_tiles(hg, bh, lo_, hi_):
                S = pair[2 + bh]
                if lo_ == 0 and bh == 0:
                    pe.wait_ge(pt_out[0], (hg + 1) * 2 * NCL)
                elif lo_ == 0:
                    pe.wait_ge(o_out, (hg + 1) * 2 * NCL)
                for t in range(lo_, hi_):
                    tt = bh * TILES + t
                    g = GROUP_OF[t]
                    if t in FIRST_OF:
                        pe.wait_ge(q_rows, (hg * 2 + bh) * NG + g + 1)
                        score_rows((0, TILES, TILES + 1)[g], S, slice(512 + g * NS, 512 + (g + 1) * NS), True, True,
                                   lambda ch, b: k_old[:, g, ch, :])
                    tile_ready(hg, tt)
                    kt = ring[:, tt % RING, :].rearrange("p (c b n) -> p c b n", c=2, b=4)
                    score_rows(t, S, slice(P + g * P, P + (g + 1) * P), t in FIRST_OF, t + 1 in FIRST_OF + (TILES,),
                               lambda ch, b: kt[:, ch, b, :]).then_inc(tile_used, 1)

            def turn_rows(hg, bh, T):
                pe.wait_ge(ss_norm, hg * 2 + bh + 1)
                for g in range(NG):
                    pe.transpose(T[:, g * P:(g + 1) * P], s_probs[:, bh, g * P:(g + 1) * P], ident[:, :])
                for g in range(NG):
                    mm = pe.transpose(T[0:NS, 512 + g * P:512 + (g + 1) * P],
                                      s_probs[:, bh, NG * P + g * NS:NG * P + (g + 1) * NS], ident[:, :])
                mm.then_inc(spt_done, 1)

            def value_tiles(hg, bh, lo_, hi_):
                if lo_ == 0 and bh:
                    pe.wait_ge(so_own, hg * 2 + 1)
                for t in range(lo_, hi_):
                    tt = (2 + bh) * TILES + t
                    if t in FIRST_OF:
                        pe.wait_ge(p_cols, (hg * 2 + bh) * (1 + NG) + 2 + GROUP_OF[t])
                    tile_ready(hg, tt)
                    for b in range(4):
                        mm = pe.matmul(C[32 * b:32 * b + 32, 0:2 * P], p_col[:, t, 32 * b:32 * b + 32],
                                       ring[:, tt % RING, b * 2 * P:(b + 1) * 2 * P],
                                       start=t == 0, stop=t == TILES - 1)
                    mm.then_inc(tile_used, 1)
                    for g in range(NG if t == 0 else 0):
                        for b in range(4):
                            pe.matmul(C[32 * b:32 * b + 32, 0:2 * P], p_new[:, g, 32 * b:32 * b + 32],
                                      v_old[:, g, :], start=False, stop=False)

            def rows_to_columns(hg, bh):
                pe.wait_ge(so_own, hg * 2 + bh + 1)
                if bh:
                    pe.wait_ge(sot_out, hg * 4 + 2)
                for ch in range(2):
                    mm = pe.matmul(C[:, 512 + ch * 4 * NQ:512 + (ch + 1) * 4 * NQ], o_own[:, ch * P:(ch + 1) * P],
                                   pick[:, :], start=True, stop=True)
                mm.then_inc(sot_done, 1)

            def mix(chunk, r):
                for h in range(2):
                    pe.wait_ge(pt_out[h], chunk * NCL + r + 1)
                if r:
                    pe.wait_ge(o_out, chunk * 4 + r)
                else:
                    pe.wait_ge(v_ready, chunk * 6 + 6)
                for c in range(6):
                    v = v_nat[:, 0, c, :] if c < 4 else v_nat[:, c - 3, r, :]
                    for h in range(2):
                        mm = pe.matmul(DD[HD * h:HD * h + HD, 0:P], v[:, HD * h:HD * h + HD],
                                       probsT[:, h, c * P:(c + 1) * P], start=c == 0, stop=c == 5)
                mm.then_inc(o_done, 1)

            def group(hg, first):
                def v_turn(ch, g, V):
                    pe.wait_ge(qkv_out, hg * U_HG + ch * U_CH + KINDS.index(("v", g)) + 1)
                    for c in range(NCL):
                        pe.transpose(V[:, c * P:(c + 1) * P], vT[:, g % 2, NS + c * P:NS + (c + 1) * P], ident[:, :])
                    pe.transpose(V[0:NS, 512:512 + P], vT[:, g % 2, 0:NS], ident[:, :]).then_inc(vt_done, 1)

                def scores(ch, u):
                    r, h = divmod(u, 2)
                    rows = slice(HD * h, HD * h + HD)
                    own = slice(NS + r * P, NS + (r + 1) * P)
                    S = score_pair(ch, u)
                    if u == 0:
                        pe.wait_ge(qkv_out, hg * U_HG + ch * U_CH + 9)
                        if first and ch:
                            pe.wait_ge(v_ready, 6 + 4)
                        elif not first and ch:
                            pe.wait_ge(p_cols, hg * 2 * (1 + NG))
                        elif not first:
                            pe.wait_ge(ss_max, hg * 2 - 1)
                    elif u == 4:
                        pe.wait_ge(pt_out[1], (hg * 2 + ch) * NCL + 1)
                    elif u > 1:
                        pe.wait_ge(s_max, (hg * 2 + ch) * 8 + (u if u < 4 else u - 1))
                    pe.matmul(S[:, 0:512], qT[rows, 0, own], kT[rows, 0, NS:NT], start=True, stop=True)
                    pe.matmul(S[:, 512:640], qT[rows, 1, own], kT[rows, 1, own], start=True, stop=True)
                    pe.matmul(S[:, 640:768], qT[rows, 2, own], kT[rows, 2, own], start=True, stop=True)\
                        .then_inc(s_done, 1)

                def turn_probs(ch, u):
                    su = (hg * 2 + ch) * 8 + u
                    pe.wait_ge(s_norm, su + 1)
                    T = turned_pair(u)
                    if u == 1:
                        pe.wait_ge(qkv_out, hg * U_HG + (ch + 1) * U_CH)
                    if T is C and (ch or u):
                        last = {0: -2, 2: 0}.get(u, u - 1)
                        pe.wait_ge(pt_out[last % 2], (hg * 2 + ch) * NCL + last // 2 + 1)
                    for c in range(6):
                        mm = pe.transpose(T[:, c * P:(c + 1) * P], probs[:, u % 2, c * P:(c + 1) * P], ident[:, :])
                    mm.then_inc(pt_done, 1)

                for ch in range(2):
                    for i in range(U_CH):
                        m = ch * U_CH + i
                        if i >= 2:
                            pe.wait_ge(qkv_out, hg * U_HG + m - 1)
                        if i in (4, 8) and not first:
                            pe.wait_ge(v_ready, (hg * 2 + ch) * 6 + i // 2)
                        unit(N_IN1 + hg * U_HG + m, m % 2, act_hi, act_lo,
                             (lambda k: pe.wait_ge(y_split[k % 2], k // 2 + 1)) if first and m == 0 else None)
                        if i == 0 and not (first and ch == 0):
                            mix(hg * 2 + ch - 1, NCL - 1)
                        if i in (3, 7):
                            if first and ch and i == 3:
                                pe.wait_ge(o_out, NCL)
                            if first and i == 7:
                                pe.wait_ge(v_ready, 6 * ch + 2)
                            v_turn(ch, i // 4, DD if first else A)
                        if first:
                            pass
                        elif ch == 0:
                            bh = i // 5
                            key_tiles(hg - 1, bh, STEP_AT[m] - bh * TILES, STEP_AT[m + 1] - bh * TILES)
                        else:
                            bh = i // 5
                            if i == 5:
                                rows_to_columns(hg - 1, 0)
                            if STEPS[m]:
                                value_tiles(hg - 1, bh, STEP_AT[m] - (2 + bh) * TILES, STEP_AT[m + 1] - (2 + bh) * TILES)
                            if i == 0:
                                pe.wait_ge(o_out, hg * 8 + 4)
                                turn_rows(hg - 1, 0, DD)
                            if i == 4:
                                turn_rows(hg - 1, 1, DD)
                        if i == 8:
                            scores(ch, 0)
                            scores(ch, 1)
                    if ch and not first:
                        rows_to_columns(hg - 1, 1)
                    scores(ch, 2)
                    if ch and not first:
                        pe.wait_ge(sot_out, hg * 4)
                    turn_probs(ch, 0)
                    turn_probs(ch, 1)
                    if ch == 0 and first:
                        pe.wait_ge(v_ready, 4)
                    elif ch == 0:
                        pe.wait_ge(ss_max, hg * 2)
                    v_turn(ch, 2, DD)
                    scores(ch, 3)
                    mix(hg * 2 + ch, 0)
                    for r in range(1, NCL - 1):
                        turn_probs(ch, 2 * r)
                        scores(ch, 2 * r + 2)
                        turn_probs(ch, 2 * r + 1)
                        scores(ch, 2 * r + 3)
                        mix(hg * 2 + ch, r)
                    turn_probs(ch, 2 * NCL - 2)
                    turn_probs(ch, 2 * NCL - 1)

            group(0, True)
            with pe.Fori(1, HG) as hg:
                group(hg, False)
            mix(KC - 1, NCL - 1)

            hg = HG - 1

            def tiles(lo_, hi_):
                for which in range(4):
                    at = [min(max(t - which * TILES, 0), TILES) for t in (lo_, hi_)]
                    if at[0] < at[1]:
                        (key_tiles if which < 2 else value_tiles)(hg, which % 2, *at)

            def prompt_unit(m):
                n, s = N_OUT1 + m, m % 2
                pe.wait_ge(w_split, LAND + n + 1)
                pe.wait_ge(res_part, KC + m + 1)
                for k in range(KC):
                    if m == 0:
                        pe.wait_ge(mid1_split[k % 2], k // 2 + 1)
                    for q, (w, x) in enumerate(((w_hi, mid1_hi), (w_hi, mid1_lo), (w_lo, mid1_hi))):
                        mm = pe.matmul(pair[s][:, 0:SEQ], w[:, s, k * P:(k + 1) * P], x[:, k, :],
                                       start=k == 0 and q == 0, stop=k == KC - 1 and q == 2)
                mm.then_inc(proj_done, 1)

            def prompt_sum(k):
                pe.wait_ge(res_done, KC + k + 1)
                mm = pe.matmul(A[:, 512:512 + SEQ], ones[:, :], res[:, k, NS:NT], start=k == 0, stop=k == KC - 1)
                if k == KC - 1:
                    mm.then_inc(ln_sum, 1)

            def prompt_squares(lo_, hi_):
                for k in range(lo_, hi_):
                    pe.wait_ge(ln_sq, 2 * KC + k + 1)
                    pe.matmul(B[:, 512:512 + SEQ], ones[:, :], sq1[:, k % 2, :], start=k == 0, stop=k == KC - 1)\
                        .then_inc(ln_sqsum, 1)

            tiles(0, TAIL_AT[1])
            for m in range(KC):
                prompt_unit(m)
                if m:
                    prompt_sum(m - 1)
                if m == 3:
                    pe.wait_ge(p_cols, (hg * 2 + 1) * (1 + NG))
                if m < KC - 1:
                    tiles(TAIL_AT[m + 1], TAIL_AT[m + 2])
                if m == 2:
                    turn_rows(hg, 0, C)
                if m == 4:
                    turn_rows(hg, 1, DD)
                if m == 6:
                    rows_to_columns(hg, 0)
            tiles(TAIL_AT[KC], 45)
            prompt_sum(KC - 1)
            tiles(45, 48)
            prompt_squares(0, 4)
            tiles(48, 50)
            prompt_squares(4, KC)
            def sample_units(units_, ks):
                at = 0 if ks[0] == 0 else 512
                for m in units_:
                    w = landing[:, m % LAND, :] if m >= LAND else ring[:, (TILES_HG + m) % RING, :]
                    if m < LAND and ks[0] == 0:
                        tile_ready(hg, TILES_HG + m)
                    for k in ks:
                        mm = pe.matmul(DD[:, at + m * NS:at + (m + 1) * NS], w[:, k * P:(k + 1) * P], res[:, k, 0:NS],
                                       start=k == ks[0], stop=k == ks[-1])
                return mm

            pe.wait_ge(p_cols, 2 * HG * (1 + NG))
            sample_units(range(LAND, KC), range(KC - 2))
            tiles(50, TILES_HG)
            rows_to_columns(hg, 1)
            sample_units(range(LAND), range(KC - 2)).then_inc(proj_done, 1)

            pe.wait_ge(sot_out, HG * 4)
            sample_units(range(KC), range(KC - 2, KC)).then_inc(proj_done, 1)
            pe.wait_ge(sample_out, 3)
            for k in range(KC):
                mm = pe.matmul(C[:, 0:NS], ones[:, :], ys[:, k, :], start=k == 0, stop=k == KC - 1)
            mm.then_inc(ln_sum, 1)
            pe.wait_ge(sample_out, 6)
            for k in range(KC):
                mm = pe.matmul(C[:, 512:512 + NS], ones[:, :], ys_sq[:, k, :], start=k == 0, stop=k == KC - 1)
            mm.then_inc(ln_sqsum, 1)

        @block.scalar
        def _(act):
            def split_hi(base, it, per, m):
                n = base + it * per + m
                act.wait_ge(w_landed[m % LAND], (base // LAND + it * (per // LAND) + m // LAND + 1) * 16)
                if m >= 2:
                    act.wait_ge(proj_done, n - 1)
                act.activation(w_hi[:, m % 2, :], landing[:, m % LAND, :], ACT.Copy).then_inc(hi_done, 1)

            def norm(round_):
                act.wait_ge(ln_sum, round_ + 1)
                act.activation(neg_mean[:, :], tok(2), ACT.Copy, scale=-1.0 / D).then_inc(ln_mean, 1)
                for k in range(KC):
                    act.wait_ge(ln_cent, KC * round_ + k + 1)
                    if k >= 2:
                        act.wait_ge(ln_sqsum, KC * round_ + k - 1)
                    act.activation(sq[:, k % 2, :], res[:, k, :], ACT.Square).then_inc(ln_sq, 1)
                act.wait_ge(ln_sqsum, KC * (round_ + 1))
                act.activation(std[:, :], tok(3), ACT.Sqrt, scale=1.0 / D, bias=vec[:, 0, V_EPS:V_EPS + 1]).then_inc(ln_std, 1)

            split_hi(0, 0, 0, 0)
            for k in range(KC):
                if k % 2 == 0:
                    act.wait_ge(x_in[k // 2], 16)
                act.activation(act_hi[:, k, :], res[:, k, :], ACT.Copy).then_inc(x_hi, 1)
                if k == 3:
                    split_hi(0, 0, 0, 1)
            act.wait_ge(consts_in[0], 16)
            act.wait_ge(made, 6)
            def products(j, ws):
                for w in ws:
                    x = u_in[:, j, w:w + SEQ]
                    if w == 0:
                        act.wait_ge(u_done, 2 * j + 4)
                        act.wait_ge(conv_merged, 2 * j + 2)
                        act.activation(pool_sum[:, j % 2, :], x, ACT.Identity, scale=vec[:, j, 0:1],
                                       bias=vec[:, j, V_DWB:V_DWB + 1]).then_inc(tap_done, 1)
                    else:
                        act.wait_ge(tap_added, j * (ACT_TAPS - 1) + w)
                        act.activation(tap_prod[:, w - 1, :], x, ACT.Copy, scale=vec[:, j, w:w + 1]).then_inc(tap_done, 1)

            for j in range(KC):
                for i in range(3):
                    n = 3 * j + i
                    split_hi(0, 0, 0, n + 2)
                    if i == 0:
                        act.wait_ge(proj_done, n + 1)
                        act.activation(sg[:, j % 2, :], tok(n % 2), ACT.Sigmoid).then_inc(gate_done, 1)
                    if i == 2:
                        act.wait_ge(proj_done, n + 1)
                        act.activation(zs[:, j, :], tok(n % 2), ACT.Copy).then_inc(z_done, 1)
                        products(j, range(3))
                    elif j:
                        products(j - 1, range(3, 6) if i == 0 else range(6, ACT_TAPS))
            products(KC - 1, range(3, ACT_TAPS))
            act.wait_ge(z_done, 1 + KC)
            for k in range(KC):
                act.activation(zs[:, k, :], zs[:, k, :], ACT.Silu).then_inc(silu_done, 1)
            act.wait_ge(u_stored, 16 * 2 * KC)
            norm(0)
            for k in range(KC + 1):
                if k < KC:
                    act.wait_ge(ln_scaled, k + 1)
                    if k >= 2:
                        act.wait_ge(gated, 2 * (k - 1))
                    act.activation(sg[:, k % 2, :], res[:, k, :], ACT.Silu, bias=vec[:, k, V_LNB:V_LNB + 1],
                                   scale=vec[:, k, V_LNG:V_LNG + 1]).then_inc(ln_act, 1)
                if k:
                    act.wait_ge(gated, 2 * k)
                    act.activation(mid_hi[:, k - 1, :], res[:, k - 1, :], ACT.Copy).then_inc(mid_hi_done, 1)

            def shifted_square(k):
                act.wait_ge(ln_cent, KC + k + 1)
                if k >= 2:
                    act.wait_ge(ln_sqsum, KC + k - 1)
                act.activation(sq[:, k % 2, :], res[:, k, :], ACT.Square).then_inc(ln_sq, 1)

            for m in range(KC):
                if m > 1:
                    shifted_square(m - 2)
                split_hi(N_OUT0, 0, 0, m + 2)
                if m == 1:
                    act.wait_ge(shift_sum, 1)
                    act.activation(shift[:, :], tok(2), ACT.Copy, scale=-1.0 / P).then_inc(shift_ready, 1)
            shifted_square(KC - 2)
            shifted_square(KC - 1)
            act.wait_ge(ln_sum, 2)
            act.activation(neg_mean[:, :], tok(2), ACT.Copy, scale=-1.0 / D).then_inc(ln_mean, 1)
            act.wait_ge(var_ready, 2)
            act.activation(std[:, :], std[:, :], ACT.Sqrt, bias=vec[:, 0, V_EPS:V_EPS + 1]).then_inc(ln_std, 1)
            for k in range(KC):
                act.wait_ge(ln_scaled, KC + k + 1)
                act.activation(res[:, k, :], res[:, k, :], ACT.Identity, bias=vec[:, k, V_B0:V_B0 + 1],
                               scale=vec[:, k, V_G0:V_G0 + 1]).then_inc(ln_act, 1)
                act.wait_ge(ln_act, KC + k + 1)
                act.activation(act_hi[:, k, :], res[:, k, :], ACT.Copy).then_inc(x_hi, 1)

            def exp_rows(hg, bh):
                act.wait_ge(ss_max, hg * 2 + bh + 1)
                act.activation(s_probs[:, bh, :], s_probs[:, bh, :], ACT.Exp, scale=-1.0,
                               bias=s_neg_top[:, bh:bh + 1], accum_out=s_total[:, bh:bh + 1]).then_inc(ss_exp, 1)

            def group(hg, first):
                for ch in range(2):
                    chunk = hg * 2 + ch

                    def exp(u):
                        act.wait_ge(s_max, chunk * 8 + u + 1)
                        act.activation(probs[:, u % 2, :], probs[:, u % 2, :], ACT.Exp, scale=-1.0,
                                       bias=neg_top[:, u % 2:u % 2 + 1],
                                       accum_out=total[:, u % 2:u % 2 + 1]).then_inc(s_exp, 1)

                    def probs_out(u):
                        act.wait_ge(pt_done, chunk * 8 + u + 1)
                        if u >= 2:
                            act.wait_ge(o_done, chunk * 4 + u // 2)
                        act.activation(probsT[:, 0, :], C[:, 0:PW], ACT.Copy).then_inc(pt_out[0], 1)

                    for i in range(U_CH):
                        m = ch * U_CH + i
                        kind, g = KINDS[i]
                        if m == 6 and not first:
                            exp_rows(hg - 1, 0)
                        if i < U_CH - 2:
                            split_hi(N_IN1, hg, U_HG, m + 2)
                        if i == U_CH - 1:
                            exp(0)
                            exp(1)
                            if ch == 0 and not first:
                                exp_rows(hg - 1, 1)
                        act.wait_ge(proj_done, N_IN1 + hg * U_HG + m + 1)
                        kept = dict(z=z_new[:, ch, :], q=q_new[:, g, ch, :], k=k_new[:, g, ch, :], v=None)[kind]
                        if m == 0 and not first:
                            act.wait_ge(handed, hg)
                        if kept is not None:
                            act.activation(kept, tok(m % 2, 0, NS), ACT.Silu if kind == "z" else ACT.Copy)
                        if kind == "z":
                            if not (first and ch == 0):
                                act.wait_ge(o_out, chunk * 4)
                            act.activation(zT[:, :], tok(m % 2), ACT.Silu).then_inc(qkv_out, 1)
                        elif kind == "q":
                            act.activation(qT[:, g, :], tok(m % 2), ACT.Copy).then_inc(qkv_out, 1)
                        elif kind == "k":
                            act.wait_ge(k_stored[g], 16 + 16 * chunk)
                            act.activation(kT[:, g, :], tok(m % 2), ACT.Copy).then_inc(qkv_out, 1)
                        else:
                            act.wait_ge(v_stored[g % 2], 16 + 16 * (chunk if g == 1 else chunk * 2 + g // 2))
                            act.activation(vT[:, g % 2, :], tok(m % 2), ACT.Copy).then_inc(qkv_out, 1)
                        if i >= U_CH - 2:
                            split_hi(N_IN1, hg, U_HG, m + 2)

                    for r in range(NCL):
                        probs_out(2 * r)
                        if r < NCL - 1:
                            exp(2 * r + 2)
                            exp(2 * r + 3)

            group(0, True)
            with act.Fori(1, HG) as hg:
                group(hg, False)
            act.wait_ge(o_out, HG * 8)
            for g in range(NG):
                act.wait_ge(k_stored[g], 16 + 16 * KC)
            act.wait_ge(v_stored[0], 16 + 16 * 2 * KC)
            act.wait_ge(v_stored[1], 16 + 16 * KC)
            for k in range(KC):
                act.activation(mid1_hi[:, k, :], res[:, k, NS:NT], ACT.Copy).then_inc(mid1_hi_done, 1)
            split_hi(N_OUT1, 0, 0, 2)
            exp_rows(HG - 1, 0)
            split_hi(N_OUT1, 0, 0, 3)
            split_hi(N_OUT1, 0, 0, 4)
            exp_rows(HG - 1, 1)
            for m in range(5, KC):
                split_hi(N_OUT1, 0, 0, m)
            act.wait_ge(ln_sum, 3)
            act.activation(neg_mean1[:, :], A[:, 512:512 + SEQ], ACT.Copy, scale=-1.0 / D).then_inc(ln_mean, 1)
            for k in range(KC):
                act.wait_ge(ln_cent, 2 * KC + k + 1)
                if k >= 2:
                    act.wait_ge(ln_sqsum, 2 * KC + k - 1)
                act.activation(sq1[:, k % 2, :], res[:, k, NS:NT], ACT.Square).then_inc(ln_sq, 1)
            act.wait_ge(ln_sqsum, 3 * KC)
            act.activation(std1[:, :], B[:, 512:512 + SEQ], ACT.Sqrt, scale=1.0 / D, bias=vec[:, 0, V_EPS:V_EPS + 1])\
                .then_inc(ln_std, 1)

            for k in range(KC):
                act.wait_ge(ln_scaled, 2 * KC + k + 1)
                act.activation(res[:, k, NS:NT], res[:, k, NS:NT], ACT.Identity, bias=vec[:, k, V_B1:V_B1 + 1],
                               scale=vec[:, k, V_G1:V_G1 + 1]).then_inc(ln_act, 1)
            act.wait_ge(ln_sum, 4)
            act.activation(neg_mean1[:, 0:NS], C[:, 0:NS], ACT.Copy, scale=-1.0 / D).then_inc(sample_out, 1)
            act.wait_ge(sample_out, 5)
            act.activation(ys_sq[:, :, :], ys[:, :, :], ACT.Square).then_inc(sample_out, 1)
            act.wait_ge(ln_sqsum, 3 * KC + 1)
            act.activation(std1[:, 0:NS], C[:, 512:512 + NS], ACT.Sqrt, scale=1.0 / D, bias=vec[:, 0, V_EPS:V_EPS + 1])\
                .then_inc(sample_out, 1)

        @block.gpsimd
        def _(pool):
            def lo(dst, src, hi):
                return pool.tensor_tensor(dst, src, hi.bitcast(F32), ALU.subtract)

            def split_lo(base, it, per, m):
                pool.wait_ge(hi_done, base + it * per + m + 1)
                lo(w_lo[:, m % 2, :], landing[:, m % LAND, :], w_hi[:, m % 2, :]).then_inc(w_split, 1)

            pool.sem_inc(w_split, LAND)
            pool.sem_inc(z_done, 1)
            pool.sem_inc(u_done, 2)
            pool.sem_inc(res_part, 2)
            pool.sem_inc(tile_used, RING)
            pool.sem_inc(tap_added, ACT_TAPS - 1)
            pool.sem_inc(conv_merged, 4)
            for s in (*k_stored, *v_stored):
                pool.sem_inc(s, 16)
            pool.memset(ones[:, :], 1.0).then_inc(made, 1)
            pool.memset(u_in[:, :, 0:HALO], 0.0).then_inc(made, 5)
            pool.wait_ge(made, 6)

            split_lo(0, 0, 0, 0)
            split_lo(0, 0, 0, 1)

            def add_taps(j, ws):
                for w in ws:
                    n = j * (ACT_TAPS - 1) + w
                    pool.wait_ge(tap_done, j * ACT_TAPS + w + 1)
                    pool.wait_ge(tap_added, n - 1 + ACT_TAPS - 1)
                    acc = pool_sum[:, j % 2, :]
                    pool.tensor_tensor(acc, acc, tap_prod[:, w - 1, :], ALU.add).then_inc(tap_added, 1)

            def sample_products(j):
                if j == 0:
                    pool.wait_ge(state_in, 16)
                    pool.wait_ge(consts_in[0], 16)
                else:
                    pool.wait_ge(sconv, 2 * j - 1)
                first = u_in[:, j, US:US + NS]
                windows = bass.AP(tensor=first.tensor, offset=first.offset, ap=[first.ap[0], [NB, W], [1, NS]])
                taps = vec[:, j, 0:W].unsqueeze(2).to_broadcast([P, W, NS])
                pool.tensor_tensor(prod[:, :, :], windows, taps, ALU.mult).then_inc(prod_done, 1)

            for j in range(KC):
                for i in range(3):
                    split_lo(0, 0, 0, 3 * j + i + 2)
                    if j and i == 0:
                        sample_products(j - 1)
                    elif j:
                        add_taps(j - 1, range(1, 4) if i == 1 else range(4, ACT_TAPS))
            sample_products(KC - 1)
            for k in range(KC):
                pool.wait_ge(mid_hi_done, k + 1)
                lo(mid_lo[:, k, :], res[:, k, :], mid_hi[:, k, :]).then_inc(mid_split, 1)
            with pool.Fori(0, 2) as it:
                for m in range(4):
                    split_lo(N_OUT0, it, 4, m + 2)
            pool.wait_ge(ln_mean, 2)
            for k in range(KC // 2, KC):
                pool.wait_ge(ln_sq, KC + k + 1)
                pool.wait_ge(ln_cent, KC + k + 1)
                pool.tensor_tensor(res[:, k, :], res[:, k, :], neg_mean[:, :], ALU.add).then_inc(off_mean[1], 1)
            for k in range(0, KC, 2):
                pool.wait_ge(x_hi, KC + k + 1)
                lo(act_lo[:, k, :], res[:, k, :], act_hi[:, k, :]).then_inc(y_split[0], 1)
            pool.wait_ge(x_hi, 2 * KC)
            pool.memset(q_row[:, :, :, :, :, :], 0.0).then_inc(rows_cleared, 1)
            pool.memset(p_col[:, :, :], 0.0).then_inc(rows_cleared, 1)
            with pool.Fori(0, HG) as hg:
                for ch in range(2):
                    for i in range(U_CH):
                        split_lo(N_IN1, hg, U_HG, ch * U_CH + i + 2)
            for k in range(0, KC, 2):
                pool.wait_ge(mid1_hi_done, k + 1)
                lo(mid1_lo[:, k, :], res[:, k, NS:NT], mid1_hi[:, k, :]).then_inc(mid1_split[0], 1)
            for m in range(2, KC):
                split_lo(N_OUT1, 0, 0, m)

        @block.vector
        def _(dve):
            def by_class(x):
                return x.rearrange("p (i c) -> p c i", c=NCL)

            def of_class(x):
                return x.rearrange("p (c i) -> p c i", c=NCL)

            def value(j):
                s = (3 * j + 1) % 2
                dve.wait_ge(proj_done, 3 * j + 2)
                dve.wait_ge(gate_done, j + 1)
                dve.tensor_tensor(u_in[:, j, US + HALO * NB:UW], tok(s, 0, NS), sg[:, j % 2, 0:NS], ALU.mult)\
                    .then_inc(u_done, 1)
                dve.tensor_tensor(by_class(u_in[:, j, HALO:US]), of_class(tok(s, NS, NT)), of_class(sg[:, j % 2, NS:NT]),
                                  ALU.mult).then_inc(u_done, 1)

            def taps(j, lo_, hi_):
                if lo_ == 0:
                    dve.wait_ge(u_done, 2 * j + 4)
                for i in range(lo_, hi_):
                    w, q = ACT_TAPS + i, j * DVE_TAPS + i
                    x, acc = u_in[:, j, w:w + SEQ], odd_sum[:, j % 2, :] if i % 2 else res[:, j, NS:NT]
                    if i < 2:
                        dve.tensor_scalar(acc, x, vec[:, j, w:w + 1], None, ALU.mult).then_inc(conv, 1)
                    else:
                        dve.wait_ge(conv, q - 1)
                        dve.scalar_tensor_tensor(out=acc, in0=x, scalar=vec[:, j, w:w + 1], in1=acc,
                                                 op0=ALU.mult, op1=ALU.add).then_inc(conv, 1)

            def merge(j):
                acc = res[:, j, NS:NT]
                last = j == KC - 1
                dve.wait_ge(conv, (j + 1) * DVE_TAPS)
                dve.tensor_tensor(acc, acc, odd_sum[:, j % 2, :], ALU.add).then_inc(conv_merged, 1)
                dve.wait_ge(conv_merged, 4 + 2 * j + 1)
                if last:
                    dve.wait_ge(pe_added, 1)
                else:
                    dve.wait_ge(tap_added, (j + 2) * (ACT_TAPS - 1))
                dve.tensor_tensor(acc, acc, A[:, 0:SEQ] if last else pool_sum[:, j % 2, :], ALU.add)\
                    .then_inc(conv_merged, 1)

            def sample_taps(j):
                dve.wait_ge(prod_done, j + 1)
                dve.tensor_reduce(res[:, j, 0:NS], prod[:, :, :].rearrange("p w n -> p n w"), mybir.AxisListType.X,
                                  ALU.add).then_inc(sconv, 1)
                dve.wait_ge(sconv, 2 * j + 1)
                dve.tensor_scalar(res[:, j, 0:NS], res[:, j, 0:NS], vec[:, j, V_DWB:V_DWB + 1], None, ALU.add)\
                    .then_inc(sconv, 1)

            def norm_begin(round_):
                dve.wait_ge(ln_mean, round_ + 1)
                for k in range(KC):
                    dve.tensor_tensor(res[:, k, :], res[:, k, :], neg_mean[:, :], ALU.add).then_inc(ln_cent, 1)
                dve.wait_ge(ln_std, round_ + 1)
                dve.reciprocal(rstd[:, :], std[:, :]).then_inc(ln_rstd, 1)
                dve.wait_ge(ln_rstd, round_ + 1)

            def norm_scale(k):
                dve.tensor_tensor(res[:, k, :], res[:, k, :], rstd[:, :], ALU.mult).then_inc(ln_scaled, 1)

            def lo(dst, src, hi):
                return dve.tensor_tensor(dst, src, hi.bitcast(F32), ALU.subtract)

            def residual(m):
                dve.wait_ge(proj_done, N_OUT0 + m + 1)
                dve.scalar_tensor_tensor(out=res[:, m, :], in0=act_hi[:, m, :].bitcast(F32), scalar=ALPHA, in1=tok(m % 2),
                                         op0=ALU.mult, op1=ALU.add).then_inc(res_part, 1)
                dve.wait_ge(res_part, m + 3)
                dve.scalar_tensor_tensor(out=res[:, m, :], in0=act_lo[:, m, :].bitcast(F32), scalar=ALPHA, in1=res[:, m, :],
                                         op0=ALU.mult, op1=ALU.add).then_inc(res_done, 1)

            for k in range(KC):
                dve.wait_ge(x_hi, k + 1)
                lo(act_lo[:, k, :], res[:, k, :], act_hi[:, k, :]).then_inc(x_split, 1)
            dve.wait_ge(made, 6)
            dve.wait_ge(consts_in[0], 16)
            dve.wait_ge(x_split, KC)
            value(0)
            for j in range(KC):
                taps(j, 0, 14)
                if j:
                    sample_taps(j - 1)
                taps(j, 14, DVE_TAPS)
                if j < KC - 1:
                    value(j + 1)
                if j:
                    merge(j - 1)
            merge(KC - 1)
            sample_taps(KC - 1)
            norm_begin(0)

            def gate(k):
                dve.wait_ge(ln_act, k + 1)
                dve.wait_ge(silu_done, k + 1)
                dve.tensor_tensor(res[:, k, 0:NS], sg[:, k % 2, 0:NS], zs[:, k, 0:NS], ALU.mult).then_inc(gated, 1)
                dve.tensor_tensor(of_class(res[:, k, NS:NT]), by_class(sg[:, k % 2, NS:NT]), of_class(zs[:, k, NS:NT]),
                                  ALU.mult).then_inc(gated, 1)

            norm_scale(0)
            norm_scale(1)
            for k in range(KC):
                gate(k)
                if k + 2 < KC:
                    norm_scale(k + 2)
            def shift_chunk(k):
                dve.wait_ge(res_done, k + 1)
                dve.tensor_tensor(res[:, k, :], res[:, k, :], shift[:, :], ALU.add).then_inc(ln_cent, 1)

            def take_mean(k):
                dve.tensor_tensor(res[:, k, :], res[:, k, :], neg_mean[:, :], ALU.add).then_inc(off_mean[0], 1)

            for m in range(KC):
                residual(m)
                if m == 1:
                    dve.wait_ge(shift_ready, 1)
                    shift_chunk(0)
                if m:
                    shift_chunk(m)
            dve.wait_ge(ln_mean, 2)
            dve.tensor_tensor(rstd[:, :], neg_mean[:, :], neg_mean[:, :], ALU.mult).then_inc(var_ready, 1)
            dve.wait_ge(var_ready, 1)
            dve.wait_ge(ln_sqsum, 2 * KC)
            dve.scalar_tensor_tensor(out=std[:, :], in0=tok(3), scalar=1.0 / D, in1=rstd[:, :],
                                     op0=ALU.mult, op1=ALU.subtract).then_inc(var_ready, 1)
            take_mean(0)
            dve.wait_ge(ln_std, 2)
            dve.reciprocal(rstd[:, :], std[:, :]).then_inc(ln_rstd, 1)
            take_mean(1)
            dve.wait_ge(ln_rstd, 2)
            for k in range(KC + 3):
                if k < KC:
                    if k < KC // 2:
                        dve.wait_ge(off_mean[0], k + 1)
                    else:
                        dve.wait_ge(off_mean[1], k + 1 - KC // 2)
                    norm_scale(k)
                    if k + 2 < KC // 2:
                        take_mean(k + 2)
                if k >= 4 and k % 2 == 0:
                    dve.wait_ge(x_hi, KC + k - 2)
                    lo(act_lo[:, k - 3, :], res[:, k - 3, :], act_hi[:, k - 3, :]).then_inc(y_split[1], 1)

            for i in range(1, 6):
                dve.wait_ge(consts_in[i], 16)
            dve.wait_ge(rows_cleared, 2)
            def q_fill(hg, bh, g):
                if bh:
                    dve.wait_ge(tile_used, RING + hg * TILES_HG + (1, 5, TILES)[g])
                for ch in range(2):
                    for half in range(2):
                        rows, h = slice(HD * half, HD * half + HD), 2 * ch + half
                        src = q_old[rows, g, ch, :].rearrange("p (q b) -> p b q", b=NB)[:, 4 * bh:4 * bh + 4, :]
                        to = lambda t: q_row[rows, t, ch, :, h, :]
                        last = dve.tensor_copy(to((0, TILES, TILES + 1)[g]), src)
                        tiles = (0, 4, 8)[g]
                        for r in range(tiles):
                            last = dve.tensor_copy(to(FIRST_OF[g] + r)[:, :, r::tiles], src[:, :, r::tiles])
                last.then_inc(q_rows, 1)

            def largest_rows(hg, bh):
                S = pair[2 + bh]
                dve.wait_ge(tile_used, RING + hg * TILES_HG + (bh + 1) * TILES)
                dve.memset(s_part[:, bh:bh + 1], 0.0)
                dve.tensor_tensor_reduce(s_probs[:, bh, :], S[:, P:P + SW], mask_s[:, bh, :], -SCALE, -NEG,
                                         ALU.add, ALU.min, s_neg_top[:, bh:bh + 1]).then_inc(ss_max, 1)

            def normalise_rows(hg, bh):
                n = hg * 2 + bh + 1
                dve.wait_ge(ss_exp, n)
                dve.reciprocal(s_part[:, bh:bh + 1], s_total[:, bh:bh + 1]).then_inc(ss_share, 1)
                dve.wait_ge(ss_share, n)
                dve.tensor_scalar(s_probs[:, bh, :], s_probs[:, bh, :], s_part[:, bh:bh + 1], None, ALU.mult)\
                    .then_inc(ss_norm, 1)

            def p_fill(hg, bh, T, g):
                if g == 0:
                    dve.wait_ge(spt_done, hg * 2 + bh + 1)
                if bh:
                    dve.wait_ge(tile_used, RING + hg * TILES_HG + 2 * TILES + (1, 5, TILES)[g])
                rows = lambda x: x.rearrange("p (m q) -> p m q", q=NQ)
                if g == 0:
                    dve.tensor_copy(p_new[:, :, :].rearrange("p g m -> p (g m)"), T[0:NS, 512:512 + NG * P])\
                        .then_inc(p_cols, 1)
                    last = dve.tensor_copy(p_col[:, 0, :], T[:, 0:P])
                tiles = (0, 4, 8)[g]
                for r in range(tiles):
                    last = dve.tensor_copy(rows(p_col[:, FIRST_OF[g] + r, :])[:, :, r::tiles],
                                           rows(T[:, g * P:(g + 1) * P])[:, :, r::tiles])
                last.then_inc(p_cols, 1)

            def own_heads(hg, bh):
                dve.wait_ge(tile_used, RING + hg * TILES_HG + (bh + 3) * TILES)
                if bh:
                    dve.wait_ge(sot_done, hg * 2 + 1)
                dve.tensor_tensor(o_own[:, :], C[:, 0:2 * P], head_mask[:, :], ALU.mult).then_inc(so_own, 1)

            def gate_rows(hg, bh):
                dve.wait_ge(sot_done, hg * 2 + bh + 1)
                for ch in range(2):
                    cols = lambda x: x.rearrange("p (q b) -> p b q", b=NB)[:, 4 * bh:4 * bh + 4, :]
                    dve.tensor_tensor(cols(res[:, bass.ds(hg * 2 + ch, 1), 0:NS].rearrange("p a n -> p (a n)")),
                                      C[:, 512 + ch * 4 * NQ:512 + (ch + 1) * 4 * NQ].rearrange("p (b q) -> p b q", b=4),
                                      cols(z_old[:, ch, :]), ALU.mult).then_inc(sot_out, 1)

            def hand_over(hg, part):
                if part == 0:
                    dve.wait_ge(qkv_out, (hg + 1) * U_HG)
                    dve.tensor_copy(q_old[:, :, :, :], q_new[:, :, :, :]).then_inc(handing, 1)
                    dve.tensor_copy(k_old[:, :, :, :], k_new[:, :, :, :]).then_inc(handing, 1)
                else:
                    dve.wait_ge(v_ready, (hg + 1) * 12)
                    dve.tensor_copy(v_old[:, :, :], v_new[:, :, :]).then_inc(handing, 1)
                    dve.tensor_copy(z_old[:, :, :], z_new[:, :, :]).then_inc(handed, 1)

            def group(hg, first):
                def v_out(ch, g):
                    V = DD if g == 2 or first else A
                    dve.wait_ge(vt_done, (hg * 2 + ch) * NG + g + 1)
                    dve.tensor_copy(v_nat[:, g, :, :].rearrange("p c n -> p (c n)"), V[:, 0:512]).then_inc(v_ready, 1)
                    dve.tensor_copy(v_new[:, g, ch * P:(ch + 1) * P], V[0:NS, 512:512 + P]).then_inc(v_ready, 1)

                def largest(ch, u):
                    su, s = (hg * 2 + ch) * 8 + u, u % 2
                    dve.wait_ge(s_done, su + 1)
                    if u >= 2:
                        dve.wait_ge(pt_done, su - 1)
                    dve.memset(share[:, s:s + 1], 0.0)
                    dve.tensor_tensor_reduce(probs[:, s, :], score_pair(ch, u)[:, 0:PW], mask_p[:, u // 2, :], -SCALE, -NEG,
                                             ALU.add, ALU.min, neg_top[:, s:s + 1]).then_inc(s_max, 1)

                def normalise(ch, u):
                    su, s = (hg * 2 + ch) * 8 + u, u % 2
                    dve.wait_ge(s_exp, su + 1)
                    dve.reciprocal(share[:, s:s + 1], total[:, s:s + 1]).then_inc(s_share, 1)
                    dve.wait_ge(s_share, su + 1)
                    dve.tensor_scalar(probs[:, s, :], probs[:, s, :], share[:, s:s + 1], None, ALU.mult)\
                        .then_inc(s_norm, 1)

                def probs_out(ch, u):
                    chunk = hg * 2 + ch
                    dve.wait_ge(pt_done, chunk * 8 + u + 1)
                    if u >= 2:
                        dve.wait_ge(o_done, chunk * 4 + u // 2)
                    dve.tensor_copy(probsT[:, 1, :], turned_pair(u)[:, 0:PW]).then_inc(pt_out[1], 1)

                def gate_out(ch, r):
                    dve.wait_ge(o_done, (hg * 2 + ch) * 4 + r + 1)
                    own = NS + r * P
                    dve.tensor_tensor(res[:, bass.ds(hg * 2 + ch, 1), own:own + P].rearrange("p a n -> p (a n)"),
                                      DD[:, 0:P], zT[:, own:own + P], ALU.mult).then_inc(o_out, 1)

                for ch in range(2):
                    chunk = hg * 2 + ch
                    if first:
                        v_out(ch, 0)
                        v_out(ch, 1)
                        largest(ch, 0)
                        largest(ch, 1)
                    elif ch == 0:
                        v_out(ch, 0)
                        largest_rows(hg - 1, 0)
                        for g in range(NG):
                            q_fill(hg - 1, 1, g)
                        v_out(ch, 1)
                        normalise_rows(hg - 1, 0)
                        largest(ch, 0)
                        largest(ch, 1)
                        largest_rows(hg - 1, 1)
                    else:
                        normalise_rows(hg - 1, 1)
                        for g in range(NG):
                            p_fill(hg - 1, 0, DD, g)
                        v_out(ch, 0)
                        own_heads(hg - 1, 0)
                        for g in range(NG):
                            p_fill(hg - 1, 1, DD, g)
                        gate_rows(hg - 1, 0)
                        v_out(ch, 1)
                        largest(ch, 0)
                        largest(ch, 1)
                        own_heads(hg - 1, 1)
                    normalise(ch, 0)
                    normalise(ch, 1)
                    if ch and not first:
                        gate_rows(hg - 1, 1)
                    for r in range(NCL):
                        if r < NCL - 1:
                            largest(ch, 2 * r + 2)
                            probs_out(ch, 2 * r + 1)
                            if r == 0:
                                v_out(ch, 2)
                            if r < NCL - 2:
                                normalise(ch, 2 * r + 2)
                                largest(ch, 2 * r + 3)
                            else:
                                largest(ch, 2 * r + 3)
                                normalise(ch, 2 * r + 2)
                            normalise(ch, 2 * r + 3)
                            gate_out(ch, r)
                        else:
                            probs_out(ch, 2 * r + 1)
                        if ch and r < 2:
                            hand_over(hg, r)
                        elif ch and r == NCL - 1:
                            dve.wait_ge(handing, 3 * (hg + 1))
                            for g in range(NG):
                                q_fill(hg, 0, g)
                    gate_out(ch, NCL - 1)

            group(0, True)
            with dve.Fori(1, HG) as hg:
                group(hg, False)
            hg = HG - 1

            def prompt_residual(m):
                dve.wait_ge(proj_done, N_OUT1 + m + 1)
                dve.scalar_tensor_tensor(out=res[:, m, NS:NT], in0=act_hi[:, m, NS:NT].bitcast(F32), scalar=ALPHA,
                                         in1=pair[m % 2][:, 0:SEQ], op0=ALU.mult, op1=ALU.add).then_inc(res_part, 1)
                dve.wait_ge(res_part, KC + m + 3)
                dve.scalar_tensor_tensor(out=res[:, m, NS:NT], in0=act_lo[:, m, NS:NT].bitcast(F32), scalar=ALPHA,
                                         in1=res[:, m, NS:NT], op0=ALU.mult, op1=ALU.add).then_inc(res_done, 1)

            for k in range(1, KC, 2):
                dve.wait_ge(mid1_hi_done, k + 1)
                lo(mid1_lo[:, k, :], res[:, k, NS:NT], mid1_hi[:, k, :]).then_inc(mid1_split[1], 1)
            dve.wait_ge(mid1_split[0], KC // 2)
            q_fill(hg, 1, 0)
            q_fill(hg, 1, 1)
            prompt_residual(0)
            largest_rows(hg, 0)
            q_fill(hg, 1, 2)
            normalise_rows(hg, 0)
            prompt_residual(1)
            prompt_residual(2)
            largest_rows(hg, 1)
            for g in range(NG):
                p_fill(hg, 0, C, g)
            prompt_residual(3)
            normalise_rows(hg, 1)
            prompt_residual(4)
            p_fill(hg, 1, DD, 0)
            p_fill(hg, 1, DD, 1)
            prompt_residual(5)
            own_heads(hg, 0)
            p_fill(hg, 1, DD, 2)
            prompt_residual(6)
            gate_rows(hg, 0)
            prompt_residual(7)
            dve.wait_ge(ln_mean, 3)
            for k in range(KC):
                dve.tensor_tensor(res[:, k, NS:NT], res[:, k, NS:NT], neg_mean1[:, :], ALU.add).then_inc(ln_cent, 1)
            own_heads(hg, 1)
            gate_rows(hg, 1)
            dve.wait_ge(ln_std, 3)
            dve.reciprocal(rstd1[:, :], std1[:, :]).then_inc(ln_rstd, 1)
            dve.wait_ge(ln_rstd, 3)
            for k in range(KC):
                dve.tensor_tensor(res[:, k, NS:NT], res[:, k, NS:NT], rstd1[:, :], ALU.mult).then_inc(ln_scaled, 1)
            over = lambda x: x[:, 0:NS].unsqueeze(1).to_broadcast([P, KC, NS])
            dve.wait_ge(proj_done, UNITS + 1)
            dve.scalar_tensor_tensor(out=ys[:, :, :], in0=act_hi[:, :, 0:NS].bitcast(F32), scalar=ALPHA,
                                     in1=DD[:, 0:KC * NS].rearrange("p (k n) -> p k n", k=KC),
                                     op0=ALU.mult, op1=ALU.add).then_inc(sample_out, 1)
            dve.wait_ge(sample_out, 1)
            dve.scalar_tensor_tensor(out=ys[:, :, :], in0=act_lo[:, :, 0:NS].bitcast(F32), scalar=ALPHA,
                                     in1=ys[:, :, :], op0=ALU.mult, op1=ALU.add).then_inc(sample_out, 1)
            dve.wait_ge(proj_done, UNITS + 2)
            dve.wait_ge(sample_out, 2)
            dve.tensor_tensor(ys[:, :, :], ys[:, :, :], DD[:, 512:512 + KC * NS].rearrange("p (k n) -> p k n", k=KC),
                              ALU.add).then_inc(sample_out, 1)
            dve.wait_ge(sample_out, 4)
            dve.tensor_tensor(ys[:, :, :], ys[:, :, :], over(neg_mean1), ALU.add).then_inc(sample_out, 1)
            dve.wait_ge(sample_out, 7)
            dve.reciprocal(rstd1[:, 0:NS], std1[:, 0:NS]).then_inc(sample_out, 1)
            dve.wait_ge(sample_out, 8)
            dve.tensor_tensor(ys[:, :, :], ys[:, :, :], over(rstd1), ALU.mult).then_inc(sample_out, 1)
            dve.wait_ge(sample_out, 9)
            for k in range(KC):
                dve.tensor_scalar(ys[:, k, :], ys[:, k, :], vec[:, k, V_G1:V_G1 + 1], vec[:, k, V_B1:V_B1 + 1],
                                  ALU.mult, ALU.add).then_inc(sample_out, 1)


def constants():
    i = np.arange(P)
    mask_p = np.full((P, NCL, PW), NEG, np.float32)
    for r in range(NCL):
        for c in range(NCL):
            back = 4 * (i[:, None] - i[None, :]) + r - c
            mask_p[:, r, c * P:(c + 1) * P][(back >= 0) & (back <= WIN[0])] = 0
        back = i[:, None] - i[None, :]
        mask_p[:, r, 4 * P:5 * P][back >= 0] = 0
        mask_p[:, r, 5 * P:6 * P][(back >= 0) & (back % 4 == 0)] = 0
    row = np.arange(P)
    b4, h, q = row // 32, row // 8 % 4, row % 8
    mask_s = np.zeros((P, 2, SW), np.float32)
    mask_s[:, :, 0:P][(i[None, :] < q[:, None])[:, None, :].repeat(2, 1)] = NEG
    mask_s[:, :, P:2 * P][(i[None, :] < q[:, None] // 4)[:, None, :].repeat(2, 1)] = NEG
    n = np.arange(NS)
    t, b = n // NB, n % NB
    for bh in range(2):
        same = b[None, :] == 4 * bh + b4[:, None]
        back = q[:, None] - t[None, :]
        for g in range(NG):
            ok = same & (back >= 0) & (back % DIL[g] == 0)
            mask_s[:, bh, NG * P + g * NS:NG * P + (g + 1) * NS][~ok] = NEG
    head_mask = (np.arange(2 * P)[None, :] // HD == h[:, None]).astype(np.float32)
    pick = np.zeros((P, 4 * NQ), np.float32)
    pick[row, b4 * NQ + q] = 1
    return dict(ident=np.eye(P, dtype=np.float32), mask_p=mask_p, mask_s=mask_s, head_mask=head_mask, pick=pick)


def units(*weights):
    return [np.ascontiguousarray(w.reshape(KC, P, P).transpose(1, 0, 2)).reshape(P, KC * P) for w in weights]


def kernel(**inputs):
    from concourse import bacc
    from concourse.bass_utils import run_bass_kernel_spmd

    x = {k: np.asarray(v) for k, v in inputs.items()}
    w0, w1 = x["conv_w_in"][0], x["attn_w_in"][0]
    cols = lambda w, at: w[:, at:at + P]
    order = [cols(w0, base + j * P) for j in range(KC) for base in (D, 0, 2 * D)]
    order += [cols(x["conv_w_out"][0], j * P) for j in range(KC)]
    place = lambda kind, g: NG * 3 if kind == "z" else 3 * g + "qkv".index(kind)
    order += [cols(w1, place(*kind) * D + j * P) for j in range(KC) for kind in KINDS]
    order += [cols(x["attn_w_out"][0], j * P) for j in range(KC)]
    arrays = dict(constants())
    arrays["w_units"] = np.stack(units(*order))

    prompt = x["x_prompt"][0].reshape(P, NCL, D).transpose(1, 0, 2).reshape(SEQ, D)
    sample = x["x_sample"].transpose(1, 0, 2).reshape(NS, D)
    chunks = lambda a: np.ascontiguousarray(a.reshape(a.shape[0], KC, P).transpose(2, 1, 0))
    arrays["xT"] = chunks(np.concatenate([sample, prompt]))
    arrays["vec"] = chunks(np.concatenate([x["conv_dw_w"][0], x["conv_dw_b"], x["conv_ln_g"], x["conv_ln_b"],
                                           x["norm_g"][0:1], x["norm_b"][0:1], x["norm_g"][1:2], x["norm_b"][1:2],
                                           np.full((1, D), EPS, np.float32)]))
    arrays["state"] = chunks(x["state_conv"][0].transpose(1, 0, 2).reshape(HALO * NB, D))
    k_tiles, v_tiles = [], []
    caches = [x[f"cache_kv_w{w}_d{dil}"][0] for w, dil in zip(WIN, DIL)]
    for g, c in enumerate(caches):
        arrays[f"cache{g}"] = c.reshape(NB, WIN[g] * 2 * D)
        c = c.reshape(2, 4, P, DIL[g], 2, HG, 2 * P)[:, :, :, 0:8]
        k_tiles.append(c[:, :, :, :, 0].reshape(2, 4, P, -1, HG, 2, P).transpose(4, 0, 3, 6, 5, 1, 2))
        v_tiles.append(c[:, :, :, :, 1].transpose(4, 0, 3, 2, 1, 5))
    arrays["k_tiles"] = np.concatenate([a.reshape(HG, 2, -1, P, 2 * 4 * P) for a in k_tiles], 2).reshape(-1, P, 2 * 4 * P)
    arrays["v_tiles"] = np.concatenate([a.reshape(HG, 2, -1, P, 2 * 4 * P) for a in v_tiles], 2).reshape(-1, P, 2 * 4 * P)

    nc = bacc.Bacc("TRN2", target_bir_lowering=False, num_devices=1)
    d = {n: nc.dram_tensor(n, a.shape, F32, kind="ExternalInput").ap() for n, a in arrays.items()}
    shapes = dict(yT=(P, KC, NT), kv_new=(KC * NG * 2, P, NT), conv_p=(P, KC, HALO), conv_s=(P, KC, HALO * NB),
                  **{f"kept{g}": (NB, (WIN[g] - NQ) * 2 * D) for g in range(NG)})
    o = {n: nc.dram_tensor(n, s, F32, kind="ExternalOutput").ap() for n, s in shapes.items()}
    build(nc, d, o)
    got = run_bass_kernel_spmd(nc, [arrays], core_ids=[0]).results[0]

    def tokens(a):
        a = np.moveaxis(a, -1, -2)
        s, p = a[..., :NS, :], a[..., NS:, :]
        p = np.swapaxes(p.reshape(*a.shape[:-2], NCL, P, D), -3, -2).reshape(*a.shape[:-2], SEQ, D)
        return p, np.swapaxes(s.reshape(*a.shape[:-2], NQ, NB, D), -3, -2)

    yp, ys = tokens(got["yT"].transpose(1, 0, 2).reshape(D, NT))
    kv = got["kv_new"].reshape(KC, NG, 2, P, NT).transpose(1, 2, 0, 3, 4).reshape(NG, 2, D, NT)
    kvp, kvs = tokens(kv)
    heads = lambda a: a.reshape(*a.shape[:-1], D // HD, HD)
    out_p, out_s = [], []
    for g in range(NG):
        keep = min(WIN[g], SEQ)
        out_p.append(heads(kvp[g].transpose(1, 0, 2))[None, None, -keep:])
        new = heads(kvs[g].transpose(1, 2, 0, 3))
        out_s.append(np.concatenate([got[f"kept{g}"].reshape(NB, WIN[g] - NQ, 2, D // HD, HD), new], 1)[None])
    conv_p = got["conv_p"].transpose(2, 1, 0).reshape(1, 1, HALO, D)
    conv_s = got["conv_s"].transpose(2, 1, 0).reshape(HALO, NB, D).transpose(1, 0, 2)[None]
    c = np.ascontiguousarray
    return (c(yp[None]), c(ys), *map(c, out_p), c(conv_p), *map(c, out_s), c(conv_s))
```
